# Optimizing a Trainium2 kernel written in Bass

```python
import math
import jax, jax.numpy as jnp
from jax import lax
import numpy as np

'''Hybrid decoder layer with Hymba-style parallel head groups.

Each layer is a single sandwich-RMSNorm residual sub-layer. One combined input projection of the
pre-normed stream feeds two token mixers side by side:
  (A) LongNet-style causal dilated sliding-window attention (NoPE). Each of its heads evaluates the
      (window, dilation) patterns (128,1), (512,4), (2048,16) with keys gathered by stride, and the
      per-pattern outputs are merged by their softmax denominators. Output multiplied by a SiLU gate.
  (B) Mamba-2 SSD mixer: causal depthwise conv on x/B/C, grouped B/C, chunked state-space scan,
      D skip, SiLU(z) output gate with grouped RMSNorm.
The branch outputs are concatenated over head groups and passed through one output projection, then
post-RMSNorm, then added to the residual stream.

Inputs: x (BATCH, SEQ, D_MODEL) float32; per-layer parameters stacked on a leading DEPTH axis.
Output: (BATCH, SEQ, D_MODEL).
'''

D_MODEL = 1024
BATCH = 1
SEQ = 2048
DEPTH = 1

D_INNER = 2 * D_MODEL
ATTN_HEADS = 16
ATTN_HEAD_DIM = 64
D_ATTN = ATTN_HEADS * ATTN_HEAD_DIM
DILATED_PATTERNS = ((128, 1), (512, 4), (2048, 16))
ATTN_BLOCK = 128
D_SSM = D_INNER - D_ATTN
SSM_HEAD_DIM = 64
SSM_HEADS = D_SSM // SSM_HEAD_DIM
SSM_GROUPS = 2
D_STATE = 128
CONV_K = 4
CHUNK = 128
D_CONV = D_SSM + 2 * SSM_GROUPS * D_STATE
D_IN_PROJ = 4 * D_ATTN + D_SSM + D_CONV + SSM_HEADS
NORM_EPS = 1e-6
DT_MIN = 1e-3
DT_MAX = 1e-1

kernel_name = 'hymba_dilated_attn_mamba2_hybrid'

def rms_norm(x, w):
    xf = x.astype(jnp.float32)
    y = xf * lax.rsqrt(jnp.mean(xf * xf, axis=-1, keepdims=True) + NORM_EPS)
    return (y * w.astype(jnp.float32)).astype(x.dtype)

def dilated_window_attention(q, k, v, window, dilation):
    b, s, h, dh = q.shape
    n = s // dilation
    nb = -(-n // ATTN_BLOCK)
    n_pad = nb * ATTN_BLOCK
    span = window // dilation

    def to_sub(t):
        t = t.reshape(b, n, dilation, h, dh).transpose(0, 2, 3, 1, 4)
        t = jnp.pad(t, ((0, 0), (0, 0), (0, 0), (0, n_pad - n), (0, 0)))
        return t.reshape(b, dilation, h, nb, ATTN_BLOCK, dh)

    def with_prev(t):
        prev = jnp.pad(t, ((0, 0), (0, 0), (0, 0), (1, 0), (0, 0), (0, 0)))[:, :, :, :-1]
        return jnp.concatenate([prev, t], axis=4)

    qb = to_sub(q)
    kw = with_prev(to_sub(k))
    vw = with_prev(to_sub(v))
    scores = jnp.einsum('bdhnqc,bdhnkc->bdhnqk', qb, kw, preferred_element_type=jnp.float32)

    qi = jnp.arange(ATTN_BLOCK)[:, None]
    kj = jnp.arange(2 * ATTN_BLOCK)[None, :]
    dist = ATTN_BLOCK + qi - kj
    key_idx = jnp.arange(nb)[:, None, None] * ATTN_BLOCK - ATTN_BLOCK + kj[None]
    valid = (dist >= 0) & (dist <= span) & (key_idx >= 0)
    scores = jnp.where(valid, scores, -jnp.inf)

    m = jnp.max(scores, axis=-1, keepdims=True)
    p = jnp.exp(scores - m)
    l = jnp.sum(p, axis=-1, keepdims=True)
    o = jnp.einsum('bdhnqk,bdhnkc->bdhnqc', p, vw.astype(jnp.float32)) / l
    lse = (m + jnp.log(l))[..., 0]

    o = o.reshape(b, dilation, h, n_pad, dh)[:, :, :, :n].transpose(0, 3, 1, 2, 4).reshape(b, s, h, dh)
    lse = lse.reshape(b, dilation, h, n_pad)[:, :, :, :n].transpose(0, 3, 1, 2).reshape(b, s, h)
    return o, lse

def mixture_of_dilations(q, k, v):
    outs, lses = [], []
    for window, dilation in DILATED_PATTERNS:
        o, lse = dilated_window_attention(q, k, v, window, dilation)
        outs.append(o)
        lses.append(lse)
    weights = jax.nn.softmax(jnp.stack(lses), axis=0)
    return jnp.einsum('pbsh,pbshd->bshd', weights, jnp.stack(outs))

def causal_depthwise_conv(x, w, bias):
    c = x.shape[-1]
    y = lax.conv_general_dilated(
        x, w[:, None, :].astype(x.dtype), window_strides=(1,), padding=[(CONV_K - 1, 0)],
        dimension_numbers=('NWC', 'WIO', 'NWC'), feature_group_count=c)
    return y + bias.astype(x.dtype)

def ssd_chunked(x, dt, a, b_mat, c_mat):
    bsz, s, h, p = x.shape
    g = SSM_GROUPS
    e = h // g
    n = b_mat.shape[-1]
    nc = s // CHUNK
    xdt = (x.astype(jnp.float32) * dt[..., None]).reshape(bsz, nc, CHUNK, g, e, p)
    a_dt = (dt * a).reshape(bsz, nc, CHUNK, g, e).transpose(0, 3, 4, 1, 2)
    bc = b_mat.astype(jnp.float32).reshape(bsz, nc, CHUNK, g, n)
    cc = c_mat.astype(jnp.float32).reshape(bsz, nc, CHUNK, g, n)
    a_cs = jnp.cumsum(a_dt, axis=-1)

    causal = jnp.tril(jnp.ones((CHUNK, CHUNK), dtype=bool))
    seg = a_cs[..., :, None] - a_cs[..., None, :]
    decay = jnp.exp(jnp.where(causal, seg, -jnp.inf))
    cb = jnp.einsum('bclgn,bcsgn->bgcls', cc, bc)
    y_diag = jnp.einsum('bgecls,bcsgep->bclgep', cb[:, :, None] * decay, xdt)

    decay_states = jnp.exp(a_cs[..., -1:] - a_cs)
    states = jnp.einsum('bclgn,bgecl,bclgep->bcgepn', bc, decay_states, xdt)

    chunk_decay = jnp.exp(a_cs[..., -1])

    def step(h_prev, inp):
        st, dec = inp
        return h_prev * dec[..., None, None] + st, h_prev

    init = jnp.zeros((bsz, g, e, p, n), jnp.float32)
    _, prev = lax.scan(step, init, (states.transpose(1, 0, 2, 3, 4, 5), chunk_decay.transpose(3, 0, 1, 2)))
    prev = prev.transpose(1, 0, 2, 3, 4, 5)

    y_off = jnp.einsum('bclgn,bcgepn,bgecl->bclgep', cc, prev, jnp.exp(a_cs))
    return (y_diag + y_off).reshape(bsz, s, h, p)

def gated_group_rms_norm(y, z, w):
    yz = y.astype(jnp.float32) * jax.nn.silu(z.astype(jnp.float32))
    shp = yz.shape
    yz = yz.reshape(shp[:-1] + (SSM_GROUPS, shp[-1] // SSM_GROUPS))
    yz = yz * lax.rsqrt(jnp.mean(yz * yz, axis=-1, keepdims=True) + NORM_EPS)
    return yz.reshape(shp) * w.astype(jnp.float32)

def hybrid_layer(hid, norm_pre_w, w_in, conv_w, conv_b, dt_bias, a_log, d_skip, ssm_norm_w, w_out, norm_post_w):
    bsz, s, _ = hid.shape
    u = rms_norm(hid, norm_pre_w)
    proj = jnp.einsum('bsd,de->bse', u, w_in.astype(u.dtype))
    sizes = [D_ATTN, D_ATTN, D_ATTN, D_ATTN, D_SSM, D_CONV]
    q, k, v, g_attn, z, xbc, dt_raw = jnp.split(proj, np.cumsum(sizes).tolist(), axis=-1)

    q = q.reshape(bsz, s, ATTN_HEADS, ATTN_HEAD_DIM) * (ATTN_HEAD_DIM ** -0.5)
    k = k.reshape(bsz, s, ATTN_HEADS, ATTN_HEAD_DIM)
    v = v.reshape(bsz, s, ATTN_HEADS, ATTN_HEAD_DIM)
    attn = mixture_of_dilations(q, k, v).reshape(bsz, s, D_ATTN)
    attn = attn * jax.nn.silu(g_attn.astype(jnp.float32))

    xbc = jax.nn.silu(causal_depthwise_conv(xbc, conv_w, conv_b))
    xs, b_mat, c_mat = jnp.split(xbc, [D_SSM, D_SSM + SSM_GROUPS * D_STATE], axis=-1)
    xs = xs.reshape(bsz, s, SSM_HEADS, SSM_HEAD_DIM)
    b_mat = b_mat.reshape(bsz, s, SSM_GROUPS, D_STATE)
    c_mat = c_mat.reshape(bsz, s, SSM_GROUPS, D_STATE)
    dt = jax.nn.softplus(dt_raw.astype(jnp.float32) + dt_bias.astype(jnp.float32))
    a = -jnp.exp(a_log.astype(jnp.float32))
    y = ssd_chunked(xs, dt, a, b_mat, c_mat) + d_skip.astype(jnp.float32)[:, None] * xs.astype(jnp.float32)
    y = gated_group_rms_norm(y.reshape(bsz, s, D_SSM), z, ssm_norm_w)

    mix = jnp.concatenate([attn, y], axis=-1).astype(hid.dtype)
    out = jnp.einsum('bse,ed->bsd', mix, w_out.astype(mix.dtype))
    return hid + rms_norm(out, norm_post_w)

def setup_inputs(seed: int = 0) -> dict:
    key = jax.random.key(seed)
    ks = jax.random.split(key, 12)
    f32 = jnp.float32
    x = jax.random.normal(ks[0], (BATCH, SEQ, D_MODEL), f32)
    norm_pre_w = 1.0 + 0.1 * jax.random.normal(ks[1], (DEPTH, D_MODEL), f32)
    w_in = jax.random.normal(ks[2], (DEPTH, D_MODEL, D_IN_PROJ), f32) * D_MODEL ** -0.5
    conv_w = jax.random.normal(ks[3], (DEPTH, CONV_K, D_CONV), f32) * CONV_K ** -0.5
    conv_b = 0.02 * jax.random.normal(ks[4], (DEPTH, D_CONV), f32)
    dt0 = jnp.exp(jax.random.uniform(ks[5], (DEPTH, SSM_HEADS), f32, math.log(DT_MIN), math.log(DT_MAX)))
    dt_bias = dt0 + jnp.log(-jnp.expm1(-dt0))
    a_log = jnp.log(jax.random.uniform(ks[6], (DEPTH, SSM_HEADS), f32, 1.0, 16.0))
    d_skip = 1.0 + 0.1 * jax.random.normal(ks[7], (DEPTH, SSM_HEADS), f32)
    ssm_norm_w = 1.0 + 0.1 * jax.random.normal(ks[8], (DEPTH, D_SSM), f32)
    w_out = jax.random.normal(ks[9], (DEPTH, D_INNER, D_MODEL), f32) * D_INNER ** -0.5
    norm_post_w = 1.0 + 0.1 * jax.random.normal(ks[10], (DEPTH, D_MODEL), f32)
    return {'x': x, 'norm_pre_w': norm_pre_w, 'w_in': w_in, 'conv_w': conv_w, 'conv_b': conv_b,
            'dt_bias': dt_bias, 'a_log': a_log, 'd_skip': d_skip, 'ssm_norm_w': ssm_norm_w,
            'w_out': w_out, 'norm_post_w': norm_post_w}

def reference(x, norm_pre_w, w_in, conv_w, conv_b, dt_bias, a_log, d_skip, ssm_norm_w, w_out, norm_post_w):
    hid = x
    for layer in range(DEPTH):
        hid = hybrid_layer(hid, norm_pre_w[layer], w_in[layer], conv_w[layer], conv_b[layer],
                           dt_bias[layer], a_log[layer], d_skip[layer], ssm_norm_w[layer],
                           w_out[layer], norm_post_w[layer])
    return hid


_drawn_inputs = setup_inputs


def setup_inputs(seed=0):
    import zlib

    import numpy as np

    out = dict(_drawn_inputs(seed))
    spreads = {}
    factors = {'conv_b': 2.979}
    for name, (base, spread) in spreads.items():
        noise = np.random.default_rng([zlib.crc32(name.encode()), seed]).standard_normal(out[name].shape)
        drawn = base * np.exp(spread * noise) if base else spread * noise
        out[name] = __import__('jax').numpy.asarray(drawn.astype(out[name].dtype))
    for name, factor in factors.items():
        out[name] = (out[name] * factor).astype(out[name].dtype)
    return out
```

```python
from contextlib import ExitStack

import numpy as np

import concourse.bass as bass
from concourse import mybir

ALU = mybir.AluOpType
ACT = mybir.ActivationFunctionType
AX = mybir.AxisListType
F32 = mybir.dt.float32
F32R = mybir.dt.float32r
I32 = mybir.dt.int32

P = 128
SEQ = 2048
D_MODEL = 1024
HEADS = 16
HEAD_DIM = 64
D_ATTN = HEADS * HEAD_DIM
D_SSM = 1024
SSM_HEADS = 16
SSM_GROUPS = 2
HEADS_PER_GROUP = SSM_HEADS // SSM_GROUPS
D_STATE = 128
CONV_K = 4
CHUNK = 128
CHUNKS = SEQ // CHUNK
D_CONV = D_SSM + 2 * SSM_GROUPS * D_STATE
D_PROJ = 4 * D_ATTN + D_SSM + D_CONV + SSM_HEADS
EPS = 1e-6

BANK = 512
KT = D_MODEL // P
TB = SEQ // BANK
TT = SEQ // P
BIG = 1e30
LN2 = float(np.log(2.0))

FT = (D_PROJ - SSM_HEADS) // P
V_COL, G_COL, Z_COL = 2 * D_ATTN, 3 * D_ATTN, 4 * D_ATTN
CONV_TILE0 = (4 * D_ATTN + D_SSM) // P
SEGMENTS = [("q", 0, 4), ("k", 4, 8), ("v", 8, 12), ("g", 12, 16), ("z", 16, 20), ("x", 20, 24), ("b", 24, 25),
            ("c", 25, 26)]
PAIRS = FT // 2
STORED = "qkgbc"
TURNED = "vzxb"
CONVOLVED = "xbc"


def before_pair(kinds, kind, pair):
    n = 0
    for k, a, b in SEGMENTS:
        if k == kind:
            return n + (pair - a if k in kinds else 0)
        if k in kinds:
            n += b - a


def total_pairs(kinds):
    return sum(b - a for k, a, b in SEGMENTS if k in kinds)


def segment_steps(eng, step):
    previous = None
    for kind, a, b in SEGMENTS:
        step(kind, a, previous)
        if b - a > 1:
            with eng.Fori(a + 1, b) as pair:
                step(kind, pair, kind)
        previous = kind
D_X0 = Z_COL + D_SSM
D_B0 = D_X0 + D_SSM
PREP = 16


def project(nc, dram, x, norm_pre_w, w_in, conv_w, conv_b):
    with ExitStack() as ctx:
        def sb(name, shape, dt=F32):
            return ctx.enter_context(nc.sbuf_tensor(name, shape, dt))

        def sem(name):
            return ctx.enter_context(nc.semaphore(name))

        n_conv = D_CONV // P
        u_hi = sb("u_hi", [P, KT, SEQ], F32R)
        u_lo = sb("u_lo", [P, KT, SEQ], F32R)
        w_raw = [sb(f"w_raw{b}", [P, KT, P]) for b in range(2)]
        w_hi = [sb(f"w_hi{b}", [P, KT, P], F32R) for b in range(2)]
        w_lo = [sb(f"w_lo{b}", [P, KT, P], F32R) for b in range(2)]
        fm = [sb(f"fm{b}", [P, SEQ]) for b in range(2)]
        conv_in = sb("conv_in", [P, CONV_K - 1 + SEQ])
        half_tanh = sb("half_tanh", [P, SEQ])
        tok = sb("tok_tile", [P, TT, P])
        ident = sb("ident", [P, P])
        tap_rows = sb("tap_rows", [(CONV_K + 1) * n_conv, P])
        taps = sb("taps", [P, (CONV_K + 1) * n_conv])
        stat = sb("stat", [P, 4, TT])
        sum_sq, root, inv_rms, eps = (stat[:, j, :] for j in range(4))
        tok_flat = tok[:, :, :].rearrange("p a b -> p (a b)")
        x_tok = [tok_flat[:, b * D_MODEL:(b + 1) * D_MODEL] for b in range(2)]
        u_tok = [half_tanh[:, b * D_MODEL:(b + 1) * D_MODEL] for b in range(2)]
        w_row = conv_in[:, 0:D_MODEL]
        squares = conv_in[:, D_MODEL:2 * D_MODEL]
        mm = [ctx.enter_context(nc.psum_tensor(f"mm{i}", [P, BANK], F32)) for i in range(TB)]
        turn = [ctx.enter_context(nc.psum_tensor(f"turn{i}", [P, BANK], F32)) for i in range(4)]

        x_in = [sem(f"x_in{b}") for b in range(2)]
        w_row_in = sem("w_row_in")
        taps_in = sem("taps_in")
        taps_turned = sem("taps_turned")
        taps_halved = sem("taps_halved")
        consts_made = sem("consts_made")
        squared = sem("squared")
        rooted = sem("rooted")
        inverted = sem("inverted")
        normed = sem("normed")
        u_turned = sem("u_turned")
        u_hi_made = sem("u_hi_made")
        u_lo_made = sem("u_lo_made")
        w_landed = [sem(f"w_landed{b}") for b in range(2)]
        w_hi_made = [sem(f"w_hi_made{b}") for b in range(2)]
        w_lo_made = [sem(f"w_lo_made{b}") for b in range(2)]
        product = [sem(f"product{i}") for i in range(TB)]
        read_out = [sem(f"read_out{i}") for i in range(TB)]
        gate_tanh = sem("gate_tanh")
        conv_tanh = sem("conv_tanh")
        conv_filled = sem("conv_filled")
        conv_step = sem("conv_step")
        padded = sem("padded")
        fm_made = [sem(f"fm_made{b}") for b in range(2)]
        fm_out = [sem(f"fm_out{b}") for b in range(2)]
        turned = sem("turned")
        tok_made = sem("tok_made")
        tok_out = sem("tok_out")
        dt_made = sem("dt_made")
        dt_out = sem("dt_out")

        w_cols = w_in.rearrange("(k p) f -> p k f", p=P)
        tok_view = dram["tok"].rearrange("(n p) f -> p n f", p=P)

        def is_first(pair):
            return isinstance(pair, int) and pair == 0

        def is_last(pair):
            return isinstance(pair, int) and pair == PAIRS - 1

        def block_cols(tb):
            return slice(tb * BANK, (tb + 1) * BANK)

        def free_fm(eng, pair, b, previous):
            if previous is not None and previous in STORED:
                eng.wait_ge(fm_out[b], (before_pair(STORED, previous, pair - 1) + 1) * 16)
            if previous is not None and previous in TURNED:
                eng.wait_ge(turned, (before_pair(TURNED, previous, pair - 1) * 2 + b + 1) * TB)

        def turned_in(kind, pair, previous):
            out = []
            if previous is not None and previous in TURNED:
                out.append((previous, pair - 1, 1))
            if kind in TURNED:
                out.append((kind, pair, 0))
            return out

        def turn_index(kind, pair, b):
            return before_pair(TURNED, kind, pair) * 2 + b

        with nc.Block() as block:
            @block.sync
            def _(sp):
                def load_w(pair, b):
                    if not is_first(pair):
                        sp.wait_ge(w_lo_made[b], pair)
                    sp.dma_start(w_raw[b][:, :, :], w_cols[:, :, bass.ds((pair * 2 + b) * P, P)])\
                      .then_inc(w_landed[b], 16)

                sp.dma_start(x_tok[0], x[0:P, :]).then_inc(x_in[0], 16)
                sp.dma_start(w_row, norm_pre_w.broadcast_to([P, D_MODEL])).then_inc(w_row_in, 16)
                sp.dma_start(x_tok[1], x[P:2 * P, :]).then_inc(x_in[1], 16)
                load_w(0, 0)
                sp.dma_start(tap_rows[0:CONV_K * n_conv, :], conv_w.rearrange("j (n p) -> (j n) p", p=P))\
                  .then_inc(taps_in, 16)
                sp.dma_start(tap_rows[CONV_K * n_conv:(CONV_K + 1) * n_conv, :],
                             conv_b.rearrange("a (n p) -> (a n) p", p=P)).then_inc(taps_in, 16)
                load_w(0, 1)
                for i in range(2, TT):
                    sp.wait_ge(normed, i - 1)
                    sp.dma_start(x_tok[i % 2], x[i * P:(i + 1) * P, :]).then_inc(x_in[i % 2], 16)

                def step(kind, pair, previous):
                    out = turned_in(kind, pair, previous)
                    for b in range(2):
                        if not is_last(pair):
                            load_w(pair + 1, b)
                        elif b == 0:
                            sp.wait_ge(w_lo_made[0], PAIRS)
                            sp.dma_start(w_raw[0][:, :, 0:SSM_HEADS], w_cols[:, :, FT * P:D_PROJ])\
                              .then_inc(w_landed[0], 16)
                        if b == 0 and out and out[0][2] == 1:
                            store_turned(*out[0])
                        if kind in STORED:
                            sp.wait_ge(fm_made[b], stored_made(kind, pair))
                            sp.dma_start(dram["feat"][bass.ds((pair * 2 + b) * P, P), :], fm[b][:, :])\
                              .then_inc(fm_out[b], 16)
                        if b == 1 and out and out[-1][2] == 0:
                            store_turned(*out[-1])

                def stored_made(kind, pair):
                    return pair + 1

                def store_turned(kind, pair, b):
                    sp.wait_ge(tok_made, (turn_index(kind, pair, b) + 1) * TB)
                    sp.dma_start(tok_view[:, :, bass.ds((pair * 2 + b) * P, P)], tok[:, :, :]).then_inc(tok_out, 16)

                segment_steps(sp, step)
                sp.wait_ge(dt_made, TB)
                sp.dma_start(dram["dt"], fm[0][0:SSM_HEADS, :]).then_inc(dt_out, 16)
                sp.wait_ge(dt_out, 16)
                for b in range(2):
                    sp.wait_ge(fm_out[b], 16 * total_pairs(STORED))
                sp.wait_ge(tok_out, 16 * 2 * total_pairs(TURNED))

            @block.gpsimd
            def _(pool):
                pool.memset(ident[:, :], 0.0).then_inc(consts_made, 1)
                pool.memset(eps, EPS).then_inc(consts_made, 1)
                pool.wait_ge(consts_made, 2)
                pool.affine_select(out=ident[:, :], in_=ident[:, :], compare_op=ALU.not_equal, fill=1.0,
                                   base=0, pattern=[[-1, P]], channel_multiplier=1).then_inc(consts_made, 1)

                def split_low(pair, b):
                    pool.wait_ge(w_hi_made[b], pair + 1)
                    pool.tensor_tensor(w_lo[b][:, :, :], w_raw[b][:, :, :], w_hi[b][:, :, :].bitcast(F32),
                                       ALU.subtract).then_inc(w_lo_made[b], 1)

                with pool.Fori(0, PAIRS) as pair:
                    for b in range(2):
                        split_low(pair, b)
                split_low(PAIRS, 0)

            @block.scalar
            def _(act):
                def split_high(pair, b):
                    act.wait_ge(w_landed[b], (pair + 1) * 16)
                    if not is_first(pair):
                        act.wait_ge(product[TB - 1], pair * 2 + b - 1)
                    act.activation(w_hi[b][:, :, :], w_raw[b][:, :, :], ACT.Copy).then_inc(w_hi_made[b], 1)

                def square(i):
                    act.wait_ge(x_in[i % 2], 16 * (i // 2 + 1))
                    act.activation(squares, x_tok[i % 2], ACT.Square, accum_out=sum_sq[:, i:i + 1])\
                       .then_inc(squared, 1)
                    act.wait_ge(squared, i + 1)
                    act.activation(root[:, i:i + 1], sum_sq[:, i:i + 1], ACT.Sqrt, bias=eps[:, 0:1],
                                   scale=1.0 / D_MODEL).then_inc(rooted, 1)

                def read_product(kind, pair, b, tb, previous):
                    act.wait_ge(product[tb], pair * 2 + b + 1)
                    if kind in "qkv":
                        if tb == 0:
                            free_fm(act, pair, b, previous)
                        done = act.activation(fm[b][:, block_cols(tb)], mm[tb][:, :], ACT.Copy,
                                              scale=-HEAD_DIM ** -0.5 if kind == "q" else 1.0)
                        done.then_inc(read_out[tb], 1)
                    elif kind in "gz":
                        act.activation(half_tanh[:, block_cols(tb)], mm[tb][:, :], ACT.Tanh, scale=0.5)\
                           .then_inc(gate_tanh, 1)
                    else:
                        if tb == 0 and (b == 1 or previous in CONVOLVED):
                            act.wait_ge(conv_step, (before_pair(CONVOLVED, kind, pair) * 2 + b) * CONV_K)
                        if tb == 0 and kind == "x" and b == 0:
                            act.wait_ge(padded, 1)
                        lo = CONV_K - 1 + tb * BANK
                        act.activation(conv_in[:, lo:lo + BANK], mm[tb][:, :], ACT.Copy).then_inc(read_out[tb], 1)

                def mark_made(kind, pair, b):
                    if kind in "qkv":
                        act.wait_ge(read_out[TB - 1], pair * 2 + b + 1)
                        act.sem_inc(fm_made[b], 1)

                act.wait_ge(consts_made, 3)
                square(0)
                split_high(0, 0)
                for i in range(TT):
                    if i + 1 < TT:
                        square(i + 1)
                    for h in range(2):
                        act.wait_ge(u_turned, 2 * i + h + 1)
                        act.activation(u_hi[:, h * 4:h * 4 + 4, i * P:(i + 1) * P],
                                       turn[2 * (i % 2) + h][:, :].rearrange("p (k t) -> p k t", t=P),
                                       ACT.Copy).then_inc(u_hi_made, 1)
                    if i % TB == TB - 1:
                        read_product("q", 0, 0, i // TB, None)
                    if i == 7:
                        split_high(0, 1)
                mark_made("q", 0, 0)

                def step(kind, pair, previous):
                    for b in range(2):
                        if is_first(pair) and b == 0:
                            continue
                        split_high(*((pair, 1) if b == 0 else (pair + 1, 0)))
                        for tb in range(TB):
                            read_product(kind, pair, b, tb, previous)
                        mark_made(kind, pair, b)
                        if kind in CONVOLVED:
                            done = before_pair(CONVOLVED, kind, pair) * 2 + b + 1
                            act.wait_ge(conv_step, done * CONV_K)
                            act.activation(half_tanh[:, :], fm[b][:, :], ACT.Tanh).then_inc(conv_tanh, 1)

                segment_steps(act, step)
                act.wait_ge(fm_out[0], 16 * total_pairs(STORED))
                for tb in range(TB):
                    act.wait_ge(product[tb], FT + 1)
                    act.activation(fm[0][0:SSM_HEADS, block_cols(tb)], mm[tb][0:SSM_HEADS, :],
                                   ACT.Copy).then_inc(dt_made, 1)

            @block.vector
            def _(dve):
                def normalise(i):
                    dve.wait_ge(rooted, i + 1)
                    dve.reciprocal(inv_rms[:, i:i + 1], root[:, i:i + 1]).then_inc(inverted, 1)
                    dve.wait_ge(inverted, i + 1)
                    if i >= 2:
                        dve.wait_ge(u_turned, 2 * (i - 1))
                    dve.scalar_tensor_tensor(out=u_tok[i % 2], in0=x_tok[i % 2], scalar=inv_rms[:, i:i + 1],
                                             in1=w_row, op0=ALU.mult, op1=ALU.mult).then_inc(normed, 1)

                dve.wait_ge(w_row_in, 16)
                normalise(0)
                for i in range(TT):
                    if i + 1 < TT:
                        normalise(i + 1)
                    for h in range(2):
                        dve.wait_ge(u_hi_made, 2 * i + h + 1)
                        part = (slice(None), slice(h * 4, h * 4 + 4), slice(i * P, (i + 1) * P))
                        dve.tensor_tensor(u_lo[part], turn[2 * (i % 2) + h][:, :].rearrange("p (k t) -> p k t", t=P),
                                          u_hi[part].bitcast(F32), ALU.subtract).then_inc(u_lo_made, 1)
                dve.wait_ge(normed, TT)
                dve.memset(conv_in[:, 0:CONV_K - 1], 0.0).then_inc(padded, 1)
                dve.wait_ge(taps_turned, 1)
                dve.tensor_scalar(taps[:, :], turn[0][:, 0:(CONV_K + 1) * n_conv], 0.5, None, ALU.mult)\
                   .then_inc(taps_halved, 1)
                dve.wait_ge(taps_halved, 1)

                def gate(kind, pair, b, previous):
                    for tb in range(TB):
                        dve.wait_ge(gate_tanh, (before_pair("gz", kind, pair) * 2 + b) * TB + tb + 1)
                        if tb == 0:
                            free_fm(dve, pair, b, previous)
                        dve.scalar_tensor_tensor(out=fm[b][:, block_cols(tb)], in0=half_tanh[:, block_cols(tb)],
                                                 scalar=1.0, in1=mm[tb][:, :], op0=ALU.add, op1=ALU.mult)\
                           .then_inc(read_out[tb], 1)
                    dve.wait_ge(read_out[TB - 1], pair * 2 + b + 1)
                    dve.sem_inc(fm_made[b], 1)

                def convolve(kind, pair, b, previous):
                    n = before_pair(CONVOLVED, kind, pair) * 2 + b
                    dve.wait_ge(read_out[TB - 1], pair * 2 + b + 1)
                    free_fm(dve, pair, b, previous)

                    def tap(j):
                        return taps[:, bass.ds(n + j * n_conv, 1)]

                    dve.tensor_scalar(fm[b][:, :], conv_in[:, 0:SEQ], tap(0), tap(CONV_K), ALU.mult, ALU.add)\
                       .then_inc(conv_step, 1)
                    for j in range(1, CONV_K):
                        dve.wait_ge(conv_step, n * CONV_K + j)
                        dve.scalar_tensor_tensor(out=fm[b][:, :], in0=conv_in[:, j:j + SEQ], scalar=tap(j),
                                                 in1=fm[b][:, :], op0=ALU.mult, op1=ALU.add).then_inc(conv_step, 1)
                    dve.wait_ge(conv_tanh, n + 1)
                    dve.scalar_tensor_tensor(out=fm[b][:, :], in0=half_tanh[:, :], scalar=1.0, in1=fm[b][:, :],
                                             op0=ALU.add, op1=ALU.mult).then_inc(fm_made[b], 1)

                def collect_turned(kind, pair, b):
                    n = turn_index(kind, pair, b)
                    for q in range(TB):
                        dve.wait_ge(turned, n * TB + q + 1)
                        if q == 0 and not (isinstance(n, int) and n == 0):
                            dve.wait_ge(tok_out, n * 16)
                        dve.tensor_copy(tok[:, q * 4:q * 4 + 4, :].rearrange("p a b -> p (a b)"), turn[q][:, :])\
                           .then_inc(tok_made, 1)

                def step(kind, pair, previous):
                    for b in range(2):
                        if kind in "gz":
                            gate(kind, pair, b, previous)
                        for k, r, bb in turned_in(kind, pair, previous):
                            if bb == 1 - b:
                                collect_turned(k, r, bb)
                        if kind in CONVOLVED:
                            convolve(kind, pair, b, previous)

                segment_steps(dve, step)

            @block.tensor
            def _(pe):
                def multiply(pair, b, tb):
                    t = pair * 2 + b
                    if tb == 0:
                        pe.wait_ge(w_lo_made[b], pair + 1)
                    if not (is_first(pair) and b == 0):
                        pe.wait_ge(read_out[tb], t)
                    for k in range(KT):
                        pe.matmul(mm[tb][:, :], w_hi[b][:, k, :], u_hi[:, k, block_cols(tb)], start=(k == 0), stop=False)
                        pe.matmul(mm[tb][:, :], w_hi[b][:, k, :], u_lo[:, k, block_cols(tb)], start=False, stop=False)
                        last = pe.matmul(mm[tb][:, :], w_lo[b][:, k, :], u_hi[:, k, block_cols(tb)],
                                         start=False, stop=(k == KT - 1))
                    last.then_inc(product[tb], 1)

                def turn_tile(kind, pair, b):
                    n = turn_index(kind, pair, b)
                    pe.wait_ge(fm_made[b], pair + 1)
                    for q in range(TB):
                        if not (isinstance(n, int) and n == 0):
                            pe.wait_ge(tok_made, (n - 1) * TB + q + 1)
                        for i in range(4):
                            tt = 4 * q + i
                            last = pe.transpose(turn[q][:, i * P:(i + 1) * P], fm[b][:, tt * P:(tt + 1) * P],
                                                ident[:, :])
                        last.then_inc(turned, 1)

                pe.wait_ge(consts_made, 3)
                for i in range(TT):
                    pe.wait_ge(normed, i + 1)
                    for h in range(2):
                        if i >= 2:
                            pe.wait_ge(u_lo_made, 2 * (i - 2) + h + 1)
                        for k in range(4):
                            last = pe.transpose(turn[2 * (i % 2) + h][:, k * P:(k + 1) * P],
                                                u_tok[i % 2][:, (h * 4 + k) * P:(h * 4 + k + 1) * P], ident[:, :])
                        last.then_inc(u_turned, 1)
                    if i % TB == TB - 1:
                        pe.wait_ge(u_lo_made, 2 * (i + 1))
                        multiply(0, 0, i // TB)
                pe.wait_ge(taps_in, 32)
                rows = (CONV_K + 1) * n_conv
                pe.transpose(turn[0][:, 0:rows], tap_rows[:, :], ident[0:rows, 0:rows]).then_inc(taps_turned, 1)

                def step(kind, pair, previous):
                    for b in range(2):
                        if not (is_first(pair) and b == 0):
                            for tb in range(TB):
                                multiply(pair, b, tb)
                        for k, r, bb in turned_in(kind, pair, previous):
                            if bb == 1 - b:
                                if kind == "v" and isinstance(pair, int):
                                    pe.wait_ge(taps_halved, 1)
                                turn_tile(k, r, bb)

                segment_steps(pe, step)
                for tb in range(TB):
                    multiply(PAIRS, 0, tb)


CLASSES = 4
CLASS_LEN = SEQ // CLASSES
CLASS_BLOCKS = CLASS_LEN // P
SPAN = 128
UNITS = CLASSES * CLASS_BLOCKS + TT
CLASS_UNITS = CLASSES * CLASS_BLOCKS
GROUP = 8
WIDE = HEAD_DIM + 2


def attend(nc, dram):
    with ExitStack() as ctx:
        def sb(name, shape, dt=F32):
            return ctx.enter_context(nc.sbuf_tensor(name, shape, dt))

        def sem(name):
            return ctx.enter_context(nc.semaphore(name))

        S_BANKS, RING = 3, 4
        ident = sb("ident_b", [P, P])
        near_mask = sb("near_mask", [P, 2 * P])
        class_mask = sb("class_mask", [P, CLASS_LEN])
        raw = {x: sb(f"raw_{x}", [P, SEQ]) for x in "qk"}
        q_parts = [sb(f"q_parts{b}", [P, SEQ], F32R) for b in range(2)]
        k_high = [sb(f"k_high{b}", [P, SEQ], F32R) for b in range(2)]
        k_rest = [sb(f"k_rest{b}", [P, SEQ], F32R) for b in range(2)]
        g = [sb(f"g{b}", [HEAD_DIM, SEQ]) for b in range(2)]
        v_nat = [sb(f"v_nat{b}", [P, TT, HEAD_DIM]) for b in range(2)]
        v_cls = [sb(f"v_cls{b}", [P, CLASS_UNITS, HEAD_DIM]) for b in range(2)]
        masked = [sb(f"masked{r}", [P, BANK]) for r in range(RING)]
        probs = [sb(f"probs{r}", [P, BANK]) for r in range(RING)]
        probs_t = [sb(f"probs_t{r}", [P, BANK]) for r in range(RING)]
        dist, rem = masked[0][:, :].bitcast(I32), masked[1][:, :].bitcast(I32)
        count, near = masked[2], masked[3]
        cls_out = [sb(f"cls_out{b}", [P, CLASS_UNITS, WIDE]) for b in range(2)]
        cls_nat = [sb(f"cls_nat{b}", [P, TT, WIDE]) for b in range(2)]
        nat_out = [sb(f"nat_out{b}", [P, TT, HEAD_DIM]) for b in range(2)]
        nat_min = [sb(f"nat_min{b}", [P, TT]) for b in range(2)]
        nat_sum = [sb(f"nat_sum{b}", [P, TT]) for b in range(2)]
        both_min = sb("both_min", [P, TT])
        drop = sb("drop", [P, 2, TT])
        weight = sb("weight", [P, 2, TT])
        part_sum = sb("part_sum", [P, 2, TT])
        denom = sb("denom", [P, TT])
        inv_denom = sb("inv_denom", [P, TT])
        scale = sb("scale", [P, 2, TT])
        part_a = sb("part_a", [P, TT, HEAD_DIM])
        part_b = sb("part_b", [P, TT, HEAD_DIM])
        merged = sb("merged", [P, TT, HEAD_DIM])
        gated = sb("gated", [HEAD_DIM, SEQ])

        ps_s = [ctx.enter_context(nc.psum_tensor(f"ps_s{i}", [P, BANK], F32)) for i in range(S_BANKS)]
        ps_t = [ctx.enter_context(nc.psum_tensor(f"ps_t{i}", [P, BANK], F32)) for i in range(2)]
        ps_o = [ctx.enter_context(nc.psum_tensor(f"ps_o{i}", [P, BANK], F32)) for i in range(2)]
        ps_x = ctx.enter_context(nc.psum_tensor("ps_x", [P, BANK], F32))

        made = sem("made")
        masks_made = sem("masks_made")
        raw_in = {x: sem(f"{x}_in") for x in "qk"}
        high_made = {x: sem(f"{x}_high_made") for x in "qk"}
        split = {x: sem(f"{x}_split") for x in "qk"}
        v_in = [sem(f"v_in{b}") for b in range(2)]
        g_in = [sem(f"g_in{b}") for b in range(2)]
        scored = sem("scored")
        masked_made = sem("masked_made")
        exped = sem("exped")
        probs_turned = sem("probs_turned")
        probs_t_made = [sem(f"probs_t_made{i}") for i in range(2)]
        weighed = sem("weighed")
        group_out = sem("group_out")
        relaid = sem("relaid")
        gate_turned = sem("gate_turned")
        gate_read_out = sem("gate_read_out")
        merge_step = sem("merge_step")
        weights_made = sem("weights_made")
        scales_made = sem("scales_made")
        pool_step = sem("pool_step")
        gated_out = sem("gated_out")
        dve_waited = sem("dve_waited")
        pe_waited = sem("pe_waited")

        def wait(eng, s, value):
            if not isinstance(value, int) or value > 0:
                eng.wait_ge(s, value)

        class Unit:

            def __init__(self, p):
                self.b, self.s = divmod(p, UNITS)
                self.group = self.s // GROUP
                if self.s < CLASS_UNITS:
                    n, c = divmod(self.s, CLASSES)
                    self.blocks = n + 1
                    self.q_cols = slice(n * BANK + c, (n + 1) * BANK, CLASSES)
                    self.k_cols = slice(c, self.blocks * BANK, CLASSES)
                    self.mask = class_mask[:, CLASS_LEN - self.blocks * P:]
                    self.v = [v_cls[self.b][:, c * CLASS_BLOCKS + j, :] for j in range(self.blocks)]
                    self.min = cls_out[self.b][:, self.s, HEAD_DIM + 1:HEAD_DIM + 2]
                    self.sum = cls_out[self.b][:, self.s, HEAD_DIM:HEAD_DIM + 1]
                else:
                    n = self.s - CLASS_UNITS
                    first = max(n - 1, 0)
                    self.blocks = n + 1 - first
                    self.q_cols = slice(n * P, (n + 1) * P)
                    self.k_cols = slice(first * P, (n + 1) * P)
                    self.mask = near_mask[:, 2 * P - self.blocks * P:]
                    self.v = [v_nat[self.b][:, j, :] for j in range(first, n + 1)]
                    self.min = nat_min[self.b][:, n:n + 1]
                    self.sum = nat_sum[self.b][:, n:n + 1]
                self.width = self.blocks * P

        STEPS = 2 * UNITS
        unit = [Unit(p) for p in range(STEPS)]
        GATE_STEP = {16: 0, 20: 1, 24: 2, 28: 3}
        MERGE_STEP = 3
        HIGH_STEPS = {4 + 3 * i: (x, i % 4) for i, x in enumerate("qqqqkkkk")}
        def loop_pairs(eng, body):
            body(0)
            with eng.Fori(1, HEADS // 2 - 1) as pair:
                body(pair)
            body(HEADS // 2 - 1)

        def is_int(x, value):
            return isinstance(x, int) and x == value

        def is_first(pair):
            return is_int(pair, 0)

        def bank_user(p):
            return next(u for u in range(p - 1, p - 2 * S_BANKS, -1) if u % STEPS % S_BANKS == p % S_BANKS)

        def has_next(pair, b):
            return not is_int(pair * 2 + b, HEADS - 1)

        def ahead(do, pair, p, n):
            if p + n < STEPS:
                do(pair, p + n)
            elif has_next(pair, 1):
                do(pair + 1, p + n - STEPS)

        def behind(do, pair, p, n):
            if p >= n:
                do(pair, p - n)
            elif not is_first(pair):
                do(pair - 1, p - n + STEPS)

        def copy_probs(eng, pair, p, copy):
            u, base = unit[p], pair * STEPS
            eng.wait_ge(probs_turned, base + p + 1)
            wait(eng, weighed, base + p - RING + 1)
            copy(probs_t[p % RING][:, 0:u.width], ps_t[p % 2][:, 0:u.width]).then_inc(probs_t_made[p % 2], 1)

        def high_of(x, b, n):
            cols = slice(n * BANK, (n + 1) * BANK)
            return (q_parts if x == "q" else k_high)[b][:, cols], raw[x][:, cols]

        def take_rest(eng, x, b):
            if x == "q":
                rest = q_parts[b][HEAD_DIM:P, :]
                ins = eng.tensor_tensor(rest, raw[x][HEAD_DIM:P, :], rest.bitcast(F32), ALU.subtract)
            else:
                ins = eng.tensor_tensor(k_rest[b][:, :], raw[x][:, :], k_high[b][:, :].bitcast(F32), ALU.subtract)
            ins.then_inc(split[x], 1)

        with nc.Block() as block:
            @block.sync
            def _(sp):
                feat, tok = dram["feat"], dram["tok"]
                v_by_class = tok.rearrange("(n i c) f -> c i n f", n=CLASS_BLOCKS, c=CLASSES)
                v_natural = tok.rearrange("(n i) f -> i n f", i=P)

                def load_qk(head):
                    for x, at in (("q", 0), ("k", D_ATTN)):
                        wait(sp, split[x], head)
                        for rows in (slice(0, HEAD_DIM), slice(HEAD_DIM, P)):
                            sp.dma_start(raw[x][rows, :], feat[bass.ds(head * HEAD_DIM + at, HEAD_DIM), :])\
                              .then_inc(raw_in[x], 16)

                def relayout(head, b):
                    sp.wait_ge(group_out, head * (UNITS // GROUP) + CLASS_UNITS // GROUP)
                    rows = P // CLASSES
                    for c in range(CLASSES):
                        for j in range(CLASSES):
                            sp.dma_start(cls_nat[b][c:P:CLASSES, j:TT:CLASSES, :],
                                         cls_out[b][j * rows:(j + 1) * rows, c:CLASS_UNITS:CLASSES, :])\
                              .then_inc(relaid, 16)

                def load_head(head, b, is_last=False):
                    wait(sp, weighed, (head - 1) * UNITS)
                    cols = bass.ds(head * HEAD_DIM + V_COL, HEAD_DIM)
                    for c in range(CLASSES):
                        sp.dma_start(v_cls[b][:, c * CLASS_BLOCKS:(c + 1) * CLASS_BLOCKS, :], v_by_class[c][:, :, cols])\
                          .then_inc(v_in[b], 16)
                    sp.dma_start(v_nat[b][:, :, :], v_natural[:, :, cols]).then_inc(v_in[b], 16)
                    if not is_int(head, 0):
                        relayout(head - 1, 1 - b)
                    if not is_last:
                        load_qk(head + 1)
                    wait(sp, gate_read_out, (head - 1) * 4)
                    sp.dma_start(g[b][:, :], feat[bass.ds(head * HEAD_DIM + G_COL, HEAD_DIM), :]).then_inc(g_in[b], 16)

                load_qk(0)
                load_head(0, 0)
                load_head(1, 1)
                with sp.Fori(1, HEADS // 2 - 1) as pair:
                    load_head(pair * 2, 0)
                    load_head(pair * 2 + 1, 1)
                load_head(HEADS - 2, 0)
                load_head(HEADS - 1, 1, is_last=True)
                relayout(HEADS - 1, 1)

            @block.gpsimd
            def _(pool):
                pool.memset(ident[:, :], 0.0).then_inc(made, 1)
                pool.memset(near_mask[:, :], 0.0).then_inc(made, 1)
                pool.iota(dist, pattern=[[-1, CLASS_LEN]], base=CLASS_LEN - P, channel_multiplier=1).then_inc(made, 1)
                pool.wait_ge(made, 3)
                pool.affine_select(out=ident[:, :], in_=ident[:, :], compare_op=ALU.not_equal, fill=1.0,
                                   base=0, pattern=[[-1, P]], channel_multiplier=1).then_inc(made, 1)
                pool.affine_select(out=near_mask[:, :], in_=near_mask[:, :], compare_op=ALU.is_ge, fill=BIG,
                                   base=0, pattern=[[1, 2 * P]], channel_multiplier=-1).then_inc(made, 1)
                pool.wait_ge(made, 5)
                pool.affine_select(out=near_mask[:, :], in_=near_mask[:, :], compare_op=ALU.is_ge, fill=BIG,
                                   base=SPAN, pattern=[[-1, 2 * P]], channel_multiplier=1).then_inc(made, 1)
                pool.wait_ge(masks_made, 7)
                pool.affine_select(out=class_mask[:, :], in_=class_mask[:, :], compare_op=ALU.is_ge, fill=BIG,
                                   base=CLASS_LEN - P, pattern=[[-1, CLASS_LEN]], channel_multiplier=1).then_inc(made, 1)

                def merge(head, b):
                    pool.wait_ge(scales_made, head + 1)
                    wait(pool, pool_step, head * 3)
                    for j, (dst, src) in enumerate(((part_a, nat_out[b][:, :, :]), (part_b, cls_nat[b][:, :, 0:HEAD_DIM]))):
                        pool.tensor_tensor(dst[:, :, :], src,
                                           scale[:, j, :].unsqueeze(2).broadcast_to([P, TT, HEAD_DIM]), ALU.mult)\
                            .then_inc(pool_step, 1)
                    pool.wait_ge(pool_step, head * 3 + 2)
                    wait(pool, gate_turned, head * 4)
                    pool.tensor_tensor(merged[:, :, :], part_a[:, :, :], part_b[:, :, :], ALU.add).then_inc(pool_step, 1)

                def store(head):
                    pool.wait_ge(gate_read_out, head * 4 + 4)
                    pool.dma_start(dram["attn"][bass.ds(head * HEAD_DIM, HEAD_DIM), :], gated[:, :])\
                        .then_inc(gated_out, 16)

                def head_turn(head, b, has_before=True, has_next=True):
                    if has_before:
                        merge(head - 1, 1 - b)
                    if has_next:
                        wait(pool, scored, head * UNITS)
                        if has_before:
                            pool.wait_ge(pool_step, head * 3)
                        for x in "qk":
                            pool.wait_ge(high_made[x], (head + 2) * TB)
                            take_rest(pool, x, 1 - b)
                            if x == "q":
                                pool.wait_ge(split[x], head + 2)
                    if has_before:
                        store(head - 1)

                head_turn(0, 0, has_before=False)
                head_turn(1, 1)
                with pool.Fori(1, HEADS // 2 - 1) as pair:
                    head_turn(pair * 2, 0)
                    head_turn(pair * 2 + 1, 1)
                head_turn(HEADS - 2, 0)
                head_turn(HEADS - 1, 1, has_next=False)
                merge(HEADS - 1, 1)
                store(HEADS - 1)
                pool.wait_ge(gated_out, 16 * HEADS)

            @block.vector
            def _(dve):
                step = [0]

                def mask_op(ins):
                    step[0] += 1
                    ins.then_inc(masks_made, 1)
                    dve.wait_ge(masks_made, step[0])

                dve.wait_ge(made, 3)
                mask_op(dve.tensor_scalar(rem, dist, CLASSES - 1, None, ALU.bitwise_and))
                mask_op(dve.tensor_scalar(count[:, :], rem, 0, None, ALU.is_equal))
                mask_op(dve.tensor_scalar(near[:, :], dist, SPAN, None, ALU.is_le))
                mask_op(dve.tensor_tensor(count[:, :], count[:, :], near[:, :], ALU.add))
                mask_op(dve.tensor_scalar(near[:, :], count[:, :], 0.0, BIG, ALU.is_equal, ALU.mult))
                mask_op(dve.tensor_scalar(class_mask[:, :], count[:, :], 2.0, -LN2, ALU.is_equal, ALU.mult))
                mask_op(dve.tensor_tensor(class_mask[:, :], class_mask[:, :], near[:, :], ALU.add))
                dve.wait_ge(made, 7)
                for x in "qk":
                    dve.wait_ge(high_made[x], TB)
                    take_rest(dve, x, 0)

                def mask(pair, p):
                    u, base = unit[p], pair * STEPS
                    dve.wait_ge(scored, base + p + 1)
                    wait(dve, exped, base + p - RING + 1)
                    if u.s == 0:
                        wait(dve, scales_made, pair * 2 + u.b - 1)
                    dve.sem_inc(dve_waited, 1)
                    dve.tensor_tensor_reduce(out=masked[p % RING][:, 0:u.width], in0=ps_s[p % S_BANKS][:, 0:u.width],
                                             in1=u.mask, scale=1.0, scalar=3e38, op0=ALU.add, op1=ALU.min,
                                             accum_out=u.min).then_inc(masked_made, 1)

                def merge_scales(head, b):
                    mins = [nat_min[b][:, :], cls_nat[b][:, :, HEAD_DIM + 1]]
                    sums = [nat_sum[b][:, :], cls_nat[b][:, :, HEAD_DIM]]
                    at = head * 9
                    dve.wait_ge(relaid, (head + 1) * CLASSES * CLASSES * 16)
                    dve.wait_ge(group_out, head * 4 + 4)
                    dve.wait_ge(exped, head * UNITS + UNITS)
                    wait(dve, pool_step, head * 3)
                    dve.tensor_tensor(both_min[:, :], mins[0], mins[1], ALU.min).then_inc(merge_step, 1)
                    dve.wait_ge(merge_step, at + 1)
                    for j in range(2):
                        dve.tensor_tensor(drop[:, j, :], mins[j], both_min[:, :], ALU.subtract).then_inc(merge_step, 1)
                    dve.wait_ge(weights_made, head + 1)
                    for j in range(2):
                        dve.tensor_tensor(part_sum[:, j, :], sums[j], weight[:, j, :], ALU.mult).then_inc(merge_step, 1)
                    dve.wait_ge(merge_step, at + 5)
                    dve.tensor_tensor(denom[:, :], part_sum[:, 0, :], part_sum[:, 1, :], ALU.add).then_inc(merge_step, 1)
                    dve.wait_ge(merge_step, at + 6)
                    dve.reciprocal(inv_denom[:, :], denom[:, :]).then_inc(merge_step, 1)
                    dve.wait_ge(merge_step, at + 7)
                    dve.tensor_tensor(scale[:, 0, :], weight[:, 0, :], inv_denom[:, :], ALU.mult).then_inc(merge_step, 1)
                    dve.tensor_tensor(scale[:, 1, :], weight[:, 1, :], inv_denom[:, :], ALU.mult).then_inc(merge_step, 1)
                    dve.wait_ge(merge_step, at + 9)
                    dve.sem_inc(scales_made, 1)

                def gate_read(n, head, b, loads):
                    dve.wait_ge(gate_turned, head * TB + n + 1)
                    if n == 0:
                        dve.wait_ge(g_in[b], loads * 16)
                        wait(dve, gated_out, head * 16)
                    cols = slice(n * BANK, (n + 1) * BANK)
                    dve.scalar_tensor_tensor(out=gated[:, cols], in0=ps_x[0:HEAD_DIM, :], scalar=0.5, in1=g[b][:, cols],
                                             op0=ALU.mult, op1=ALU.mult).then_inc(gate_read_out, 1)

                def copy_odd(pair, p):
                    copy_probs(dve, pair, p, lambda o, i: dve.tensor_copy(o, i))

                def side(pair, p):
                    b, s = divmod(p, UNITS)
                    if is_first(pair) and b == 0:
                        return
                    if s == MERGE_STEP:
                        merge_scales(pair * 2 + b - 1, 1 - b)
                    if s in GATE_STEP:
                        gate_read(GATE_STEP[s], pair * 2 + b - 1, 1 - b, pair + b)

                def body(pair):
                    if is_first(pair):
                        mask(pair, 0)
                        mask(pair, 1)
                    for p in range(STEPS):
                        ahead(mask, pair, p, 2)
                        if p % 2:
                            copy_odd(pair, p)
                        side(pair, p)

                loop_pairs(dve, body)
                merge_scales(HEADS - 1, 1)
                for n in range(4):
                    gate_read(n, HEADS - 1, 1, HEADS // 2)

            @block.scalar
            def _(act):
                def take_high(x, b, n, head):
                    if n == 0:
                        act.wait_ge(raw_in[x], (head + 1) * 32)
                        wait(act, scored, (head - 1) * UNITS)
                    dst, src = high_of(x, b, n)
                    act.activation(dst, src, ACT.Copy).then_inc(high_made[x], 1)

                for x in "qk":
                    for n in range(TB):
                        take_high(x, 0, n, 0)

                def exponentiate(pair, p):
                    u, base = unit[p], pair * STEPS
                    if u.s == 0:
                        wait(act, scales_made, pair * 2 + u.b - 1)
                    act.wait_ge(masked_made, base + p + 1)
                    wait(act, probs_turned, base + p - RING + 1)
                    act.activation(probs[p % RING][:, 0:u.width], masked[p % RING][:, 0:u.width], ACT.Exp,
                                   bias=u.min, scale=-1.0, accum_out=u.sum).then_inc(exped, 1)

                def group_read(pair, p):
                    u = unit[p]
                    act.wait_ge(weighed, pair * STEPS + p + 1)
                    at = (u.group % 2) * GROUP
                    dst = (cls_out[u.b][:, at:at + GROUP, 0:HEAD_DIM] if u.s < CLASS_UNITS
                           else nat_out[u.b][:, at:at + GROUP, :])
                    if u.group == 2:
                        wait(act, pool_step, (pair * 2 + u.b - 1) * 3)
                    act.activation(dst, ps_o[u.group % 2][:, :].rearrange("p (u f) -> p u f", f=HEAD_DIM), ACT.Copy)                       .then_inc(group_out, 1)

                def weights(head):
                    act.wait_ge(merge_step, head * 9 + 3)
                    act.activation(weight[:, :, :], drop[:, :, :], ACT.Exp, scale=-1.0).then_inc(weights_made, 1)

                def side(pair, p):
                    b, s = divmod(p, UNITS)
                    if (p - 2) % GROUP == 0:
                        behind(group_read, pair, p, 3)
                    if s == MERGE_STEP and not (is_first(pair) and b == 0):
                        weights(pair * 2 + b - 1)
                    if s in HIGH_STEPS and has_next(pair, b):
                        x, n = HIGH_STEPS[s]
                        take_high(x, 1 - b, n, pair * 2 + b + 1)

                def body(pair):
                    if is_first(pair):
                        exponentiate(pair, 0)
                    for p in range(STEPS):
                        ahead(exponentiate, pair, p, 1)
                        if p % 2 == 0:
                            copy_probs(act, pair, p, lambda o, i: act.activation(o, i, ACT.Copy))
                        side(pair, p)

                loop_pairs(act, body)
                group_read(HEADS // 2 - 1, STEPS - 1)
                weights(HEADS - 1)

            @block.tensor
            def _(pe):
                def score(pair, p):
                    u, base = unit[p], pair * STEPS
                    if u.s == 0:
                        pe.wait_ge(split["q"], pair * 2 + u.b + 1)
                        pe.wait_ge(split["k"], pair * 2 + u.b + 1)
                    wait(pe, masked_made, base + bank_user(p) + 1)
                    bank = ps_s[p % S_BANKS][:, 0:u.width]
                    pe.matmul(bank, q_parts[u.b][:, u.q_cols], k_high[u.b][:, u.k_cols], start=True, stop=False)
                    pe.matmul(bank, q_parts[u.b][:, u.q_cols], k_rest[u.b][:, u.k_cols], start=False, stop=True)\
                      .then_inc(scored, 1)

                def turn_probs(pair, p):
                    u, base = unit[p], pair * STEPS
                    pe.wait_ge(exped, base + p + 1)
                    wait(pe, probs_t_made[p % 2], pair * (STEPS // 2) + p // 2)
                    for j in range(u.blocks):
                        last = pe.transpose(ps_t[p % 2][:, j * P:(j + 1) * P], probs[p % RING][:, j * P:(j + 1) * P],
                                            ident[:, :])
                    last.then_inc(probs_turned, 1)

                def weigh(pair, p):
                    u = unit[p]
                    if u.s == 0:
                        pe.wait_ge(v_in[u.b], (pair + 1) * (CLASSES + 1) * 16)
                    pe.wait_ge(probs_t_made[p % 2], pair * (STEPS // 2) + p // 2 + 1)
                    if u.s % GROUP == 0:
                        wait(pe, group_out, pair * (STEPS // GROUP) + p // GROUP - 1)
                    for j in range(u.blocks):
                        last = pe.matmul(ps_o[u.group % 2][:, (u.s % GROUP) * HEAD_DIM:(u.s % GROUP + 1) * HEAD_DIM],
                                         probs_t[p % RING][:, j * P:(j + 1) * P], u.v[j],
                                         start=(j == 0), stop=(j == u.blocks - 1))
                    last.then_inc(weighed, 1)

                def turn_merged(n, head):
                    pe.wait_ge(pool_step, (head + 1) * 3)
                    wait(pe, gate_read_out, head * TB + n)
                    pe.sem_inc(pe_waited, 1)
                    for j in range(TT // TB):
                        last = pe.transpose(ps_x[0:HEAD_DIM, j * P:(j + 1) * P], merged[:, n * 4 + j, :], ident[:, :])
                    last.then_inc(gate_turned, 1)

                def side(pair, p):
                    b, s = divmod(p, UNITS)
                    if s in GATE_STEP and not (is_first(pair) and b == 0):
                        turn_merged(GATE_STEP[s], pair * 2 + b - 1)

                def body(pair):
                    if is_first(pair):
                        for p in range(3):
                            score(pair, p)
                    for p in range(STEPS):
                        ahead(score, pair, p, 3)
                        turn_probs(pair, p)
                        behind(weigh, pair, p, 2)
                        side(pair, p)

                pe.wait_ge(made, 7)
                loop_pairs(pe, body)
                for p in range(STEPS - 2, STEPS):
                    weigh(HEADS // 2 - 1, p)
                for n in range(TB):
                    turn_merged(n, HEADS - 1)


def scan_and_project(nc, dram, x, w_out, dt_bias, a_log, d_skip, ssm_norm_w, norm_post_w, out):
    with ExitStack() as ctx:
        def sb(name, shape, dt=F32):
            return ctx.enter_context(nc.sbuf_tensor(name, shape, dt))

        def sem(name):
            return ctx.enter_context(nc.semaphore(name))

        def ps(name):
            return ctx.enter_context(nc.psum_tensor(name, [P, BANK], F32))

        KO = 2 * D_MODEL // P
        KA = D_ATTN // P
        SEGS = P // SSM_HEADS
        SEG_LEN = SEQ // SEGS
        HD = SSM_HEADS * HEAD_DIM
        GW = HEADS_PER_GROUP * HEAD_DIM

        ident = sb("ident_c", [P, P])
        causal = sb("causal", [P, P])
        wo_hi = sb("wo_hi", [P, KO, D_MODEL], F32R)
        wo_lo = sb("wo_lo", [P, KO, D_MODEL], F32R)
        mix_hi = sb("mix_hi", [P, KO, P], F32R)
        mix_lo = sb("mix_lo", [P, KO, P], F32R)
        post_w = sb("post_w", [P, D_MODEL])
        norm_w = sb("norm_w", [P, KA])
        skip = sb("skip", [P, SSM_HEADS])
        cum_b = sb("cum_b", [P, SSM_HEADS, CHUNK])
        decay = sb("decay", [P, SSM_HEADS, CHUNK])
        xs = sb("xs", [P, SSM_HEADS, HEAD_DIM])
        x_dt = sb("x_dt", [P, SSM_HEADS, HEAD_DIM])
        y = sb("y", [P, SSM_HEADS, HEAD_DIM])
        z2 = sb("z2", [P, HD])
        b_tok = sb("b_tok", [P, SSM_GROUPS, D_STATE])
        bc_t = sb("bc_t", [P, 2 * SSM_GROUPS, CHUNK])
        state = sb("state", [P, SSM_HEADS, HEAD_DIM])
        attn_t = sb("attn_t", [P, KA, P])
        x_res = sb("x_res", [P, D_MODEL])
        o_tok = sb("o_tok", [P, D_MODEL])
        cb = sb("cb", [P, SSM_GROUPS, CHUNK])
        cum_tok = sb("cum_tok", [P, CHUNKS, SSM_HEADS])
        dt_tok = sb("dt_tok", [P, CHUNKS, SSM_HEADS])
        small = sb("small", [P, 3, SSM_HEADS])
        grown = sb("grown", [P, 3, SSM_HEADS])
        ssq = sb("ssq", [P, 4])
        mean = sb("mean", [P, 4])
        rstd = sb("rstd", [P, 4])
        minus_half = sb("minus_half", [P, 4])
        flat = [decay[:, 2 * i:2 * i + 2, :].rearrange("p a b -> p (a b)") for i in range(8)]
        dt_raw, size, expd, one_plus, log1, gap, is_tiny, keep = flat
        dt, cum = (cum_b[:, 2 * i:2 * i + 2, :].rearrange("p a b -> p (a b)") for i in range(2))
        wo_raw = [x_res[:, :], o_tok[:, :]]
        cols = sb("cols", [P, 4])

        ps_cb = ps("ps_cb")
        ps_state = [ps("ps_state0"), ps("ps_state1")]
        ps_turn = ps_state
        ps_y = [ps("ps_y0"), ps("ps_y1")]
        ps_out = [ps("ps_out0"), ps("ps_out1")]

        names = ("made dt_in cols_in rows_in prep prep_act cum_stored tok_turned tok_made wo_scaled wo_hi_made "
                 "wo_lo_made xs_in z_in b_in bc_in cum_in attn_in x_in small_made grown_made seg_made seg_bounded decayed cb_done "
                 "cb_made weighed_made x_dt_made x_end_made skipped states_done off_done y_off_made state_faded "
                 "state_made y_skip diag_done y_diag_made y_gated y_squared y_rstd y_scaled y_turned mix_hi_made "
                 "mix_lo_made attn_hi_made attn_lo_made out_done out_squared out_rstd out_scaled out_added stored "
                 "mean_made root_made pool_waited").split()
        S = {n: sem("c_" + n) for n in names}
        wo_in = [sem(f"c_wo_in{b}") for b in range(2)]

        def wait(eng, name, value):
            if not isinstance(value, int) or value > 0:
                eng.wait_ge(S[name], value)

        def chunks(eng, body):
            for c in range(3):
                body(c)
            with eng.Fori(3, CHUNKS) as c:
                body(c)

        def has(c):
            return not isinstance(c, int) or c >= 0

        group = [slice(g * GW, (g + 1) * GW) for g in range(SSM_GROUPS)]
        heads_of = [slice(g * HEADS_PER_GROUP, (g + 1) * HEADS_PER_GROUP) for g in range(SSM_GROUPS)]
        y_flat = y[:, :, :].rearrange("p h d -> p (h d)")

        def spread(ap, n):
            return ap.unsqueeze(2).broadcast_to([P, ap.shape[1], n])

        with nc.Block() as block:
            @block.sync
            def _(sp):
                by_segment = "h (s j) -> s h j"
                sp.dma_start(dt_raw, dram["dt"].rearrange(by_segment, s=SEGS)).then_inc(S["dt_in"], 16)
                for j, src in enumerate((dt_bias, a_log)):
                    for s in range(SEGS):
                        sp.dma_start(cols[s * SSM_HEADS:(s + 1) * SSM_HEADS, j:j + 1], src.rearrange("a h -> h a"),
                                     allow_slow_non_contiguous=True).then_inc(S["cols_in"], 16)
                sp.dma_start(skip[:, :], d_skip.broadcast_to([P, SSM_HEADS])).then_inc(S["rows_in"], 16)
                sp.dma_start(post_w[:, :], norm_post_w.broadcast_to([P, D_MODEL])).then_inc(S["rows_in"], 16)
                sp.dma_start(norm_w[:, :], ssm_norm_w.rearrange("a (n p) -> p (a n)", p=P),
                             allow_slow_non_contiguous=True).then_inc(S["rows_in"], 16)

                def load(c):
                    tokens = bass.ds(c * CHUNK, CHUNK)
                    wait(sp, "seg_made", c)
                    wait(sp, "small_made", c)
                    sp.dma_start(cum_b[:, :, :], dram["cum"][:, tokens].unsqueeze(0).broadcast_to([P, SSM_HEADS, CHUNK]))\
                      .then_inc(S["cum_in"], 16)
                    wait(sp, "cb_done", c)
                    wait(sp, "off_done", c)
                    sp.dma_start(bc_t[:, :, :], dram["feat"][D_B0:D_B0 + 4 * P, :]
                                 .rearrange("(q n) t -> n q t", n=P)[:, :, tokens]).then_inc(S["bc_in"], 16)
                    wait(sp, "states_done", c)
                    sp.dma_start(b_tok[:, :, :].rearrange("p g n -> p (g n)"), dram["tok"][tokens, D_B0:D_B0 + 2 * P])\
                      .then_inc(S["b_in"], 16)
                    wait(sp, "y_skip", c)
                    sp.dma_start(xs[:, :, :].rearrange("p h d -> p (h d)"), dram["tok"][tokens, D_X0:D_X0 + D_SSM])\
                      .then_inc(S["xs_in"], 16)
                    wait(sp, "y_gated", c)
                    sp.dma_start(z2[:, :], dram["tok"][tokens, Z_COL:Z_COL + D_SSM]).then_inc(S["z_in"], 16)
                    wait(sp, "attn_lo_made", c)
                    sp.dma_start(attn_t[:, :, :], dram["attn"].rearrange("(k p) t -> p k t", p=P)[:, :, tokens])\
                      .then_inc(S["attn_in"], 16)

                wait(sp, "prep", PREP)
                sp.dma_start(dram["cum"].rearrange(by_segment, s=SEGS), cum).then_inc(S["cum_stored"], 16)
                for t in range(KO):
                    if t >= 2:
                        sp.wait_ge(S["wo_lo_made"], t - 1)
                    sp.dma_start(wo_raw[t % 2], w_out[t * P:(t + 1) * P, :]).then_inc(wo_in[t % 2], 16)
                    if t == 3:
                        sp.wait_ge(S["cum_stored"], 16)
                        sp.wait_ge(S["tok_turned"], 1)
                        load(0)
                with sp.Fori(1, CHUNKS) as c:
                    load(c)

            @block.gpsimd
            def _(pool):
                pool.memset(ident[:, :], 0.0).then_inc(S["made"], 1)
                pool.memset(causal[:, :], 1.0).then_inc(S["made"], 1)
                pool.memset(minus_half[:, :], -0.5).then_inc(S["made"], 1)
                pool.memset(state[:, :, :], 0.0).then_inc(S["made"], 1)
                pool.wait_ge(S["made"], 4)
                pool.affine_select(out=ident[:, :], in_=ident[:, :], compare_op=ALU.not_equal, fill=1.0,
                                   base=0, pattern=[[-1, P]], channel_multiplier=1).then_inc(S["made"], 1)
                pool.affine_select(out=causal[:, :], in_=causal[:, :], compare_op=ALU.is_ge, fill=0.0,
                                   base=0, pattern=[[1, P]], channel_multiplier=-1).then_inc(S["made"], 1)
                pool.wait_ge(S["rows_in"], 48)
                pool.wait_ge(S["tok_made"], 2)

                def residual(c):
                    wait(pool, "out_added", c)
                    pool.dma_start(x_res[:, :], x[bass.ds(c * CHUNK, CHUNK), :]).then_inc(S["x_in"], 16)

                def store(c):
                    pool.wait_ge(S["out_added"], c + 1)
                    pool.dma_start(out[bass.ds(c * CHUNK, CHUNK), :], o_tok[:, :]).then_inc(S["stored"], 16)

                def finish_output(c):
                    pool.wait_ge(S["out_squared"], 2 * (c + 1))
                    pool.tensor_tensor(mean[:, 2:3], ssq[:, 2:3], ssq[:, 3:4], ALU.add).then_inc(S["root_made"], 1)
                    pool.wait_ge(S["root_made"], 2 * c + 1)
                    pool.sem_inc(S["pool_waited"], 1)
                    pool.tensor_scalar(mean[:, 3:4], mean[:, 2:3], 1.0 / D_MODEL, EPS, ALU.mult, ALU.add)\
                        .then_inc(S["root_made"], 1)
                    pool.wait_ge(S["root_made"], 2 * c + 2)
                    pool.tensor_tensor(rstd[:, 2:3], mean[:, 3:4], minus_half[:, 2:3], ALU.pow).then_inc(S["out_rstd"], 1)
                    pool.wait_ge(S["out_scaled"], 2 * (c + 1))
                    pool.wait_ge(S["x_in"], 16 * (c + 1))
                    pool.tensor_tensor(o_tok[:, :], o_tok[:, :], x_res[:, :], ALU.add).then_inc(S["out_added"], 1)

                def body(c):
                    pool.wait_ge(S["xs_in"], (c + 1) * 16)
                    wait(pool, "diag_done", c)
                    pool.tensor_tensor(x_dt[:, :, :], xs[:, :, :], spread(dt_of(c), HEAD_DIM), ALU.mult)\
                        .then_inc(S["x_dt_made"], 1)
                    pool.wait_ge(S["grown_made"], c + 1)
                    pool.wait_ge(S["x_dt_made"], c + 1)
                    wait(pool, "y_turned", c)
                    pool.tensor_tensor(y[:, :, :], x_dt[:, :, :], spread(grown[:, 1, :], HEAD_DIM), ALU.mult)\
                        .then_inc(S["x_end_made"], 1)
                    pool.wait_ge(S["off_done"], c + 1)
                    wait(pool, "state_made", c)
                    pool.tensor_tensor(state[:, :, :], state[:, :, :], spread(grown[:, 0, :], HEAD_DIM), ALU.mult)\
                        .then_inc(S["state_faded"], 1)
                    pool.tensor_tensor(xs[:, :, :], xs[:, :, :], spread(skip[:, :], HEAD_DIM), ALU.mult)\
                        .then_inc(S["skipped"], 1)
                    if has(c - 2):
                        finish_output(c - 2)
                        store(c - 2)
                        residual(c - 1)
                    pool.wait_ge(S["y_squared"], 2 * (c + 1))
                    pool.sem_inc(S["pool_waited"], 1)
                    pool.tensor_scalar(mean[:, 0:2], ssq[:, 0:2], 1.0 / GW, EPS, ALU.mult, ALU.add)\
                        .then_inc(S["mean_made"], 1)
                    pool.wait_ge(S["mean_made"], c + 1)
                    pool.tensor_tensor(rstd[:, 0:2], mean[:, 0:2], minus_half[:, 0:2], ALU.pow).then_inc(S["y_rstd"], 1)
                    wait(pool, "out_done", c * 2)
                    pool.wait_ge(S["attn_hi_made"], c + 1)
                    pool.tensor_tensor(mix_lo[:, 0:KA, :], attn_t[:, :, :], mix_hi[:, 0:KA, :].bitcast(F32),
                                       ALU.subtract).then_inc(S["attn_lo_made"], 1)

                def dt_of(c):
                    return dt_tok[:, bass.ds(c, 1), :].rearrange("p a h -> p (a h)")

                pool.wait_ge(S["wo_lo_made"], KO)
                residual(0)
                chunks(pool, body)
                for c in (CHUNKS - 2, CHUNKS - 1):
                    finish_output(c)
                    store(c)
                    if c < CHUNKS - 1:
                        residual(c + 1)
                pool.wait_ge(S["stored"], 16 * CHUNKS)

            @block.vector
            def _(dve):
                n = [0]

                def prep(ins):
                    n[0] += 1
                    ins.then_inc(S["prep"], 1)
                    dve.wait_ge(S["prep"], n[0])

                dve.wait_ge(S["dt_in"], 16)
                dve.wait_ge(S["cols_in"], 2 * SEGS * 16)
                prep(dve.tensor_scalar(dt_raw, dt_raw, cols[:, 0:1], None, ALU.add))
                prep(dve.scalar_tensor_tensor(out=size, in0=dt_raw, scalar=-1.0, in1=dt_raw, op0=ALU.mult, op1=ALU.max))
                dve.wait_ge(S["prep_act"], 1)
                prep(dve.tensor_scalar(one_plus, expd, 1.0, None, ALU.add))
                prep(dve.tensor_scalar(gap, one_plus, -1.0, None, ALU.add))
                prep(dve.tensor_scalar(is_tiny, gap, 0.0, None, ALU.is_equal))
                prep(dve.tensor_tensor(gap, gap, is_tiny, ALU.add))
                prep(dve.reciprocal(gap, gap))
                prep(dve.tensor_tensor(gap, gap, expd, ALU.mult))
                dve.wait_ge(S["prep_act"], 3)
                prep(dve.tensor_tensor(gap, gap, log1, ALU.mult))
                prep(dve.tensor_tensor(is_tiny, is_tiny, expd, ALU.mult))
                prep(dve.tensor_tensor(gap, gap, is_tiny, ALU.add))
                prep(dve.scalar_tensor_tensor(out=dt, in0=dt_raw, scalar=0.0, in1=gap, op0=ALU.max, op1=ALU.add))
                prep(dve.tensor_scalar(size, dt, cols[:, 2:3], -1.0, ALU.mult, ALU.mult))
                prep(dve.memset(keep, 1.0))
                prep(dve.memset(keep.rearrange("p (a b) -> p a b", b=CHUNK)[:, :, 0:1], 0.0))
                prep(dve.tensor_tensor_scan(cum, keep, size, 0.0, ALU.mult, ALU.add))
                assert n[0] == PREP
                for j, dst in enumerate((cum_tok, dt_tok)):
                    dve.wait_ge(S["tok_turned"], 1)
                    dve.tensor_copy(dst[:, :, :].rearrange("p (s a) h -> p a s h", a=2),
                                    ps_y[j][:, 0:2 * P].rearrange("p (a s h) -> p a s h", a=2, h=SSM_HEADS))\
                       .then_inc(S["tok_made"], 1)

                for t in range(KO):
                    dve.wait_ge(wo_in[t % 2], 16 * (t // 2 + 1))
                    if t == KA:
                        dve.wait_ge(S["rows_in"], 48)
                    if t >= KA:
                        dve.tensor_scalar(wo_raw[t % 2], wo_raw[t % 2], norm_w[:, t - KA:t - KA + 1], None, ALU.mult)\
                           .then_inc(S["wo_scaled"], 1)
                    dve.wait_ge(S["wo_hi_made"], t + 1)
                    dve.tensor_tensor(wo_lo[:, t, :], wo_raw[t % 2], wo_hi[:, t, :].bitcast(F32), ALU.subtract)\
                       .then_inc(S["wo_lo_made"], 1)

                def out_scale(c):
                    dve.wait_ge(S["out_rstd"], c + 1)
                    for h in range(2):
                        half = slice(h * BANK, (h + 1) * BANK)
                        dve.scalar_tensor_tensor(out=o_tok[:, half], in0=o_tok[:, half], scalar=rstd[:, 2:3],
                                                 in1=post_w[:, half], op0=ALU.mult, op1=ALU.mult)\
                           .then_inc(S["out_scaled"], 1)

                def body(c):
                    cum_c = cum_tok[:, bass.ds(c, 1), :].rearrange("p a h -> p (a h)")
                    dve.wait_ge(S["cum_in"], (c + 1) * 16)
                    dve.wait_ge(S["tok_made"], 2)
                    wait(dve, "grown_made", c)
                    last = cum_b[:, :, CHUNK - 1:CHUNK].rearrange("p h a -> p (h a)")
                    dve.tensor_copy(small[:, 0, :], last)
                    dve.tensor_tensor(small[:, 1, :], last, cum_c, ALU.subtract)
                    dve.tensor_copy(small[:, 2, :], cum_c).then_inc(S["small_made"], 1)
                    wait(dve, "diag_done", c)
                    dve.tensor_tensor(decay[:, :, :], cum_b[:, :, :], spread(cum_c, CHUNK), ALU.subtract)\
                       .then_inc(S["seg_made"], 1)
                    dve.wait_ge(S["seg_made"], c + 1)
                    dve.tensor_scalar(decay[:, :, :], decay[:, :, :], 0.0, None, ALU.min).then_inc(S["seg_bounded"], 1)
                    dve.wait_ge(S["cb_done"], c + 1)
                    dve.tensor_tensor(cb[:, :, :], ps_cb[:, 0:SSM_GROUPS * CHUNK].rearrange("p (g l) -> p g l", l=CHUNK),
                                      causal[:, :].unsqueeze(1).broadcast_to([P, SSM_GROUPS, CHUNK]), ALU.mult)\
                       .then_inc(S["cb_made"], 1)
                    dve.wait_ge(S["decayed"], c + 1)
                    dve.wait_ge(S["cb_made"], c + 1)
                    for g in range(SSM_GROUPS):
                        dve.tensor_tensor(decay[:, heads_of[g], :], decay[:, heads_of[g], :],
                                          cb[:, g, :].unsqueeze(1).broadcast_to([P, HEADS_PER_GROUP, CHUNK]),
                                          ALU.mult).then_inc(S["weighed_made"], 1)
                    if has(c - 2):
                        out_scale(c - 2)
                    dve.wait_ge(S["off_done"], c + 1)
                    dve.wait_ge(S["states_done"], c + 1)
                    dve.wait_ge(S["grown_made"], c + 1)
                    for g in range(SSM_GROUPS):
                        dve.tensor_tensor(y[:, heads_of[g], :], ps_y[g][:, :].rearrange("p (h d) -> p h d", d=HEAD_DIM),
                                          spread(grown[:, 2, heads_of[g]], HEAD_DIM), ALU.mult).then_inc(S["y_off_made"], 1)
                    dve.wait_ge(S["state_faded"], c + 1)
                    for g in range(SSM_GROUPS):
                        st = state[:, heads_of[g], :].rearrange("p h d -> p (h d)")
                        done = dve.tensor_tensor(st, st, ps_state[g][:, :], ALU.add)
                    done.then_inc(S["state_made"], 1)
                    dve.wait_ge(S["skipped"], c + 1)
                    dve.wait_ge(S["y_off_made"], 2 * (c + 1))
                    dve.tensor_tensor(y[:, :, :], y[:, :, :], xs[:, :, :], ALU.add).then_inc(S["y_skip"], 1)
                    dve.wait_ge(S["diag_done"], c + 1)
                    dve.wait_ge(S["y_skip"], c + 1)
                    for g in range(SSM_GROUPS):
                        done = dve.tensor_tensor(y_flat[:, group[g]], y_flat[:, group[g]], ps_y[g][:, :], ALU.add)
                    done.then_inc(S["y_diag_made"], 1)
                    dve.wait_ge(S["y_diag_made"], c + 1)
                    dve.wait_ge(S["z_in"], (c + 1) * 16)
                    dve.scalar_tensor_tensor(out=y_flat, in0=y_flat, scalar=0.5, in1=z2[:, :], op0=ALU.mult,
                                             op1=ALU.mult).then_inc(S["y_gated"], 1)
                    for h in range(2):
                        dve.wait_ge(S["mix_hi_made"], 2 * c + h + 1)
                        at = slice(KA + 4 * h, KA + 4 * h + 4)
                        dve.tensor_tensor(mix_lo[:, at, :], ps_turn[h][:, :].rearrange("p (k t) -> p k t", t=P),
                                          mix_hi[:, at, :].bitcast(F32), ALU.subtract).then_inc(S["mix_lo_made"], 1)

                chunks(dve, body)
                out_scale(CHUNKS - 2)
                out_scale(CHUNKS - 1)

            @block.scalar
            def _(act):
                act.wait_ge(S["cols_in"], 2 * SEGS * 16)
                act.wait_ge(S["prep"], 2)
                act.activation(expd, size, ACT.Exp, scale=-1.0).then_inc(S["prep_act"], 1)
                act.activation(cols[:, 2:3], cols[:, 1:2], ACT.Exp).then_inc(S["prep_act"], 1)
                act.wait_ge(S["prep"], 3)
                act.activation(log1, one_plus, ACT.Ln).then_inc(S["prep_act"], 1)
                for t in range(KO):
                    act.wait_ge(wo_in[t % 2], 16 * (t // 2 + 1))
                    if t >= KA:
                        act.wait_ge(S["wo_scaled"], t - KA + 1)
                    act.activation(wo_hi[:, t, :], wo_raw[t % 2], ACT.Copy).then_inc(S["wo_hi_made"], 1)

                def out_read(c, h):
                    act.wait_ge(S["out_done"], 2 * c + h + 1)
                    if h == 0:
                        wait(act, "stored", c * 16)
                    act.activation(o_tok[:, h * BANK:(h + 1) * BANK], ps_out[h][:, :], ACT.Copy)
                    act.activation(ps_out[h][:, :], ps_out[h][:, :], ACT.Square,
                                   accum_out=ssq[:, 2 + h:3 + h]).then_inc(S["out_squared"], 1)

                def body(c):
                    act.wait_ge(S["small_made"], c + 1)
                    wait(act, "state_faded", c)
                    act.activation(grown[:, :, :], small[:, :, :], ACT.Exp).then_inc(S["grown_made"], 1)
                    act.wait_ge(S["seg_bounded"], c + 1)
                    act.activation(decay[:, :, :], decay[:, :, :], ACT.Exp).then_inc(S["decayed"], 1)
                    if has(c - 1):
                        out_read(c - 1, 0)
                    act.wait_ge(S["y_gated"], c + 1)
                    for g in range(SSM_GROUPS):
                        wait(act, "y_skip", c + 1)
                        act.activation(x_dt_junk(g), y_flat[:, group[g]], ACT.Square, accum_out=ssq[:, g:g + 1])\
                           .then_inc(S["y_squared"], 1)
                    act.wait_ge(S["y_rstd"], c + 1)
                    for g in range(SSM_GROUPS):
                        act.activation(y_flat[:, group[g]], y_flat[:, group[g]], ACT.Copy, scale=rstd[:, g:g + 1])\
                           .then_inc(S["y_scaled"], 1)
                    act.wait_ge(S["attn_in"], (c + 1) * 16)
                    wait(act, "out_done", c * 2)
                    act.activation(mix_hi[:, 0:KA, :], attn_t[:, :, :], ACT.Copy).then_inc(S["attn_hi_made"], 1)
                    for h in range(2):
                        act.wait_ge(S["y_turned"], c + 1)
                        act.activation(mix_hi[:, KA + 4 * h:KA + 4 * h + 4, :],
                                       ps_turn[h][:, :].rearrange("p (k t) -> p k t", t=P), ACT.Copy)\
                           .then_inc(S["mix_hi_made"], 1)
                    if has(c - 1):
                        out_read(c - 1, 1)

                def x_dt_junk(g):
                    return x_dt[:, heads_of[g], :].rearrange("p h d -> p (h d)")

                chunks(act, body)
                for h in range(2):
                    out_read(CHUNKS - 1, h)

            @block.tensor
            def _(pe):
                pe.wait_ge(S["made"], 6)
                pe.wait_ge(S["prep"], PREP)
                for j, src in enumerate((cum, dt)):
                    for a in range(2):
                        last = pe.transpose(ps_y[j][:, a * P:(a + 1) * P], src[:, a * P:(a + 1) * P], ident[:, :])
                last.then_inc(S["tok_turned"], 1)
                pe.wait_ge(S["tok_made"], 2)
                pe.wait_ge(S["wo_lo_made"], KO)

                def project_half(c, h):
                    if h == 0:
                        pe.wait_ge(S["attn_lo_made"], c + 1)
                    wait(pe, "out_squared", 2 * (c - 1) + h + 1)
                    cols_h = slice(h * BANK, (h + 1) * BANK)
                    for kk in range(KO):
                        if h == 0 and kk == KA:
                            pe.wait_ge(S["mix_lo_made"], 2 * (c + 1))
                        pe.matmul(ps_out[h][:, :], mix_hi[:, kk, :], wo_hi[:, kk, cols_h], start=(kk == 0), stop=False)
                        pe.matmul(ps_out[h][:, :], mix_hi[:, kk, :], wo_lo[:, kk, cols_h], start=False, stop=False)
                        last = pe.matmul(ps_out[h][:, :], mix_lo[:, kk, :], wo_hi[:, kk, cols_h],
                                         start=False, stop=(kk == KO - 1))
                    last.then_inc(S["out_done"], 1)

                def body(c):
                    pe.wait_ge(S["bc_in"], (c + 1) * 16)
                    wait(pe, "cb_made", c)
                    for g in range(SSM_GROUPS):
                        last = pe.matmul(ps_cb[:, g * CHUNK:(g + 1) * CHUNK], bc_t[:, g, :], bc_t[:, SSM_GROUPS + g, :],
                                         start=True, stop=True)
                    last.then_inc(S["cb_done"], 1)
                    wait(pe, "state_made", c)
                    wait(pe, "y_diag_made", c)
                    for g in range(SSM_GROUPS):
                        last = pe.matmul(ps_y[g][:, :], bc_t[:, SSM_GROUPS + g, :],
                                         state[:, heads_of[g], :].rearrange("p h d -> p (h d)"), start=True, stop=True)
                    last.then_inc(S["off_done"], 1)
                    if has(c - 1):
                        project_half(c - 1, 0)
                    pe.wait_ge(S["b_in"], (c + 1) * 16)
                    pe.wait_ge(S["x_end_made"], c + 1)
                    wait(pe, "mix_lo_made", 2 * c)
                    for g in range(SSM_GROUPS):
                        last = pe.matmul(ps_state[g][:, :], b_tok[:, g, :],
                                         y[:, heads_of[g], :].rearrange("p h d -> p (h d)"), start=True, stop=True)
                    last.then_inc(S["states_done"], 1)
                    pe.wait_ge(S["x_dt_made"], c + 1)
                    pe.wait_ge(S["weighed_made"], 2 * (c + 1))
                    pe.wait_ge(S["y_off_made"], 2 * (c + 1))
                    for h in range(SSM_HEADS):
                        at = (h % HEADS_PER_GROUP) * HEAD_DIM
                        last = pe.matmul(ps_y[h // HEADS_PER_GROUP][:, at:at + HEAD_DIM], decay[:, h, :], x_dt[:, h, :],
                                         start=True, stop=True)
                    last.then_inc(S["diag_done"], 1)
                    if has(c - 1):
                        project_half(c - 1, 1)
                    pe.wait_ge(S["y_scaled"], 2 * (c + 1))
                    pe.wait_ge(S["state_made"], c + 1)
                    for kk in range(KA):
                        last = pe.transpose(ps_turn[kk // 4][:, (kk % 4) * P:(kk % 4 + 1) * P],
                                            y_flat[:, kk * P:(kk + 1) * P], ident[:, :])
                    last.then_inc(S["y_turned"], 1)

                chunks(pe, body)
                for h in range(2):
                    project_half(CHUNKS - 1, h)


def hybrid_layer_kernel(nc, x, norm_pre_w, w_in, conv_w, conv_b, dt_bias, a_log, d_skip, ssm_norm_w, w_out,
                        norm_post_w, out):
    def scratch(name, shape):
        return nc.dram_tensor(name, shape, F32, kind="Internal").ap()

    dram = {
        "feat": scratch("feat", (FT * P, SEQ)),
        "tok": scratch("tok", (SEQ, FT * P)),
        "dt": scratch("dt_scratch", (SSM_HEADS, SEQ)),
        "cum": scratch("cum_scratch", (SSM_HEADS, SEQ)),
        "attn": scratch("attn", (D_ATTN, SEQ)),
    }
    project(nc, dram, x[0], norm_pre_w, w_in[0], conv_w[0], conv_b)
    attend(nc, dram)
    scan_and_project(nc, dram, x[0], w_out[0], dt_bias, a_log, d_skip, ssm_norm_w, norm_post_w, out[0])


_INS = ["x", "norm_pre_w", "w_in", "conv_w", "conv_b", "dt_bias", "a_log", "d_skip", "ssm_norm_w", "w_out",
        "norm_post_w"]


def kernel(**inputs):
    import numpy as _np
    import concourse.bacc as _bacc
    from concourse import mybir as _mybir
    from concourse.bass_utils import run_bass_kernel_spmd as _run

    nc = _bacc.Bacc("TRN2", target_bir_lowering=False, num_devices=1)
    arrays, args = {}, []
    for name in _INS:
        a = _np.ascontiguousarray(inputs[name])
        arrays[f"in_{name}_dram"] = a
        args.append(nc.dram_tensor(f"in_{name}_dram", a.shape, _mybir.dt.from_np(a.dtype), kind="ExternalInput").ap())
    args.append(nc.dram_tensor("out_dram", (1, SEQ, D_MODEL), F32, kind="ExternalOutput").ap())
    hybrid_layer_kernel(nc, *args)
    r = _run(nc, [arrays], core_ids=[0])
    return r.results[0]["out_dram"]
```

```python
from contextlib import ExitStack

import numpy as np

import concourse.bass as bass
from concourse import mybir

ALU = mybir.AluOpType
ACT = mybir.ActivationFunctionType
F32 = mybir.dt.float32
F32R = mybir.dt.float32r
I32 = mybir.dt.int32

P = 128
SEQ = 2048
D_MODEL = 1024
HEADS = 16
HEAD_DIM = 64
D_ATTN = HEADS * HEAD_DIM
D_SSM = 1024
SSM_HEADS = 16
SSM_GROUPS = 2
HEADS_PER_GROUP = SSM_HEADS // SSM_GROUPS
D_STATE = 128
CONV_K = 4
CHUNK = 128
CHUNKS = SEQ // CHUNK
D_CONV = D_SSM + 2 * SSM_GROUPS * D_STATE
D_PROJ = 4 * D_ATTN + D_SSM + D_CONV + SSM_HEADS
EPS = 1e-6

BANK = 512
KT = D_MODEL // P
TB = SEQ // BANK
TT = SEQ // P
BIG = 1e30
LN2 = float(np.log(2.0))

FT = (D_PROJ - SSM_HEADS) // P
V_COL, G_COL, Z_COL = 2 * D_ATTN, 3 * D_ATTN, 4 * D_ATTN
SEGMENTS = [("q", 0, 4), ("k", 4, 8), ("v", 8, 12), ("g", 12, 16), ("z", 16, 20), ("x", 20, 24), ("b", 24, 25),
            ("c", 25, 26)]
PAIRS = FT // 2
STORED = "qkgbc"
TURNED = "vzxb"
CONVOLVED = "xbc"


def before_pair(kinds, kind, pair):
    n = 0
    for k, a, b in SEGMENTS:
        if k == kind:
            return n + (pair - a if k in kinds else 0)
        if k in kinds:
            n += b - a


def total_pairs(kinds):
    return sum(b - a for k, a, b in SEGMENTS if k in kinds)


def segment_steps(eng, step):
    previous = None
    for kind, a, b in SEGMENTS:
        step(kind, a, previous)
        if b - a > 1:
            with eng.Fori(a + 1, b) as pair:
                step(kind, pair, kind)
        previous = kind


D_X0 = Z_COL + D_SSM
D_B0 = D_X0 + D_SSM


def project(nc, dram, x, norm_pre_w, w_in, conv_w, conv_b):
    with ExitStack() as ctx:
        def sb(name, shape, dt=F32):
            return ctx.enter_context(nc.sbuf_tensor(name, shape, dt))

        def sem(name):
            return ctx.enter_context(nc.semaphore(name))

        n_conv = D_CONV // P
        u_hi = sb("u_hi", [P, KT, SEQ], F32R)
        u_lo = sb("u_lo", [P, KT, SEQ], F32R)
        w_raw = [sb(f"w_raw{b}", [P, KT, P]) for b in range(2)]
        w_hi = [sb(f"w_hi{b}", [P, KT, P], F32R) for b in range(2)]
        w_lo = [sb(f"w_lo{b}", [P, KT, P], F32R) for b in range(2)]
        fm = [sb(f"fm{b}", [P, SEQ]) for b in range(2)]
        conv_in = sb("conv_in", [P, CONV_K - 1 + SEQ])
        half_tanh = sb("half_tanh", [P, SEQ])
        tok = sb("tok_tile", [P, TT, P])
        ident = sb("ident", [P, P])
        tap_rows = sb("tap_rows", [(CONV_K + 1) * n_conv, P])
        taps = sb("taps", [P, (CONV_K + 1) * n_conv])
        stat = sb("stat", [P, 4, TT])
        sum_sq, root, inv_rms, eps = (stat[:, j, :] for j in range(4))
        tok_flat = tok[:, :, :].rearrange("p a b -> p (a b)")
        x_tok = [tok_flat[:, b * D_MODEL:(b + 1) * D_MODEL] for b in range(2)]
        u_tok = [half_tanh[:, b * D_MODEL:(b + 1) * D_MODEL] for b in range(2)]
        w_row = conv_in[:, 0:D_MODEL]
        squares = conv_in[:, D_MODEL:2 * D_MODEL]
        mm = [ctx.enter_context(nc.psum_tensor(f"mm{i}", [P, BANK], F32)) for i in range(TB)]
        turn = [ctx.enter_context(nc.psum_tensor(f"turn{i}", [P, BANK], F32)) for i in range(4)]

        x_in = [sem(f"x_in{b}") for b in range(2)]
        w_row_in = sem("w_row_in")
        taps_in = sem("taps_in")
        taps_turned = sem("taps_turned")
        taps_halved = sem("taps_halved")
        consts_made = sem("consts_made")
        squared = sem("squared")
        rooted = sem("rooted")
        inverted = sem("inverted")
        normed = sem("normed")
        u_turned = sem("u_turned")
        u_hi_made = sem("u_hi_made")
        u_lo_made = sem("u_lo_made")
        w_landed = [sem(f"w_landed{b}") for b in range(2)]
        w_hi_made = [sem(f"w_hi_made{b}") for b in range(2)]
        w_lo_made = [sem(f"w_lo_made{b}") for b in range(2)]
        product = [sem(f"product{i}") for i in range(TB)]
        read_out = [sem(f"read_out{i}") for i in range(TB)]
        gate_tanh = sem("gate_tanh")
        conv_tanh = sem("conv_tanh")
        conv_filled = sem("conv_filled")
        conv_step = sem("conv_step")
        padded = sem("padded")
        fm_made = [sem(f"fm_made{b}") for b in range(2)]
        fm_out = [sem(f"fm_out{b}") for b in range(2)]
        turned = sem("turned")
        tok_made = sem("tok_made")
        tok_out = sem("tok_out")
        dt_made = sem("dt_made")
        dt_out = sem("dt_out")

        w_cols = w_in.rearrange("(k p) f -> p k f", p=P)
        tok_view = dram["tok"].rearrange("(n p) f -> p n f", p=P)

        def is_first(pair):
            return isinstance(pair, int) and pair == 0

        def is_last(pair):
            return isinstance(pair, int) and pair == PAIRS - 1

        EARLY = {3: (0, 0), 5: (1, 0), 7: (0, 1), 9: (1, 1), 11: (0, 2), 13: (1, 2)}

        def block_cols(tb):
            return slice(tb * BANK, (tb + 1) * BANK)

        def free_fm(eng, pair, b, previous):
            if previous is not None and previous in STORED:
                eng.wait_ge(fm_out[b], (before_pair(STORED, previous, pair - 1) + 1) * 16)
            if previous is not None and previous in TURNED:
                eng.wait_ge(turned, (before_pair(TURNED, previous, pair - 1) * 2 + b + 1) * TB)

        def turned_in(kind, pair, previous):
            out = []
            if previous is not None and previous in TURNED:
                out.append((previous, pair - 1, 1))
            if kind in TURNED:
                out.append((kind, pair, 0))
            return out

        def turn_index(kind, pair, b):
            return before_pair(TURNED, kind, pair) * 2 + b

        with nc.Block() as block:
            @block.sync
            def _(sp):
                def load_w(pair, b):
                    if not is_first(pair):
                        sp.wait_ge(w_lo_made[b], pair)
                    sp.dma_start(w_raw[b][:, :, :], w_cols[:, :, bass.ds((pair * 2 + b) * P, P)])\
                      .then_inc(w_landed[b], 16)

                sp.dma_start(x_tok[0], x[0:P, :]).then_inc(x_in[0], 16)
                sp.dma_start(w_row, norm_pre_w.broadcast_to([P, D_MODEL])).then_inc(w_row_in, 16)
                sp.dma_start(x_tok[1], x[P:2 * P, :]).then_inc(x_in[1], 16)
                load_w(0, 0)
                sp.dma_start(tap_rows[0:CONV_K * n_conv, :], conv_w.rearrange("j (n p) -> (j n) p", p=P))\
                  .then_inc(taps_in, 16)
                sp.dma_start(tap_rows[CONV_K * n_conv:(CONV_K + 1) * n_conv, :],
                             conv_b.rearrange("a (n p) -> (a n) p", p=P)).then_inc(taps_in, 16)
                load_w(0, 1)
                for i in range(2, TT):
                    sp.wait_ge(normed, i - 1)
                    sp.dma_start(x_tok[i % 2], x[i * P:(i + 1) * P, :]).then_inc(x_in[i % 2], 16)

                def step(kind, pair, previous):
                    out = turned_in(kind, pair, previous)
                    for b in range(2):
                        if not is_last(pair):
                            load_w(pair + 1, b)
                        elif b == 0:
                            sp.wait_ge(w_lo_made[0], PAIRS)
                            sp.dma_start(w_raw[0][:, :, 0:SSM_HEADS], w_cols[:, :, FT * P:D_PROJ])\
                              .then_inc(w_landed[0], 16)
                        if b == 0 and out and out[0][2] == 1:
                            store_turned(*out[0])
                        if kind in STORED:
                            sp.wait_ge(fm_made[b], pair + 1)
                            sp.dma_start(dram["feat"][bass.ds((pair * 2 + b) * P, P), :], fm[b][:, :])\
                              .then_inc(fm_out[b], 16)
                        if b == 1 and out and out[-1][2] == 0:
                            store_turned(*out[-1])

                def store_turned(kind, pair, b):
                    sp.wait_ge(tok_made, (turn_index(kind, pair, b) + 1) * TB)
                    sp.dma_start(tok_view[:, :, bass.ds((pair * 2 + b) * P, P)], tok[:, :, :]).then_inc(tok_out, 16)

                segment_steps(sp, step)
                sp.wait_ge(dt_made, TB)
                sp.dma_start(dram["dt"], fm[0][0:SSM_HEADS, :]).then_inc(dt_out, 16)
                sp.wait_ge(dt_out, 16)
                for b in range(2):
                    sp.wait_ge(fm_out[b], 16 * total_pairs(STORED))
                sp.wait_ge(tok_out, 16 * 2 * total_pairs(TURNED))

            @block.gpsimd
            def _(pool):
                pool.memset(ident[:, :], 0.0).then_inc(consts_made, 1)
                pool.memset(eps, EPS).then_inc(consts_made, 1)
                pool.wait_ge(consts_made, 2)
                pool.affine_select(out=ident[:, :], in_=ident[:, :], compare_op=ALU.not_equal, fill=1.0,
                                   base=0, pattern=[[-1, P]], channel_multiplier=1).then_inc(consts_made, 1)

                def split_low(pair, b):
                    pool.wait_ge(w_hi_made[b], pair + 1)
                    pool.tensor_tensor(w_lo[b][:, :, :], w_raw[b][:, :, :], w_hi[b][:, :, :].bitcast(F32),
                                       ALU.subtract).then_inc(w_lo_made[b], 1)

                with pool.Fori(0, PAIRS) as pair:
                    for b in range(2):
                        split_low(pair, b)
                split_low(PAIRS, 0)

            @block.scalar
            def _(act):
                def split_high(pair, b):
                    act.wait_ge(w_landed[b], (pair + 1) * 16)
                    if not is_first(pair):
                        act.wait_ge(product[TB - 1], pair * 2 + b - 1)
                    act.activation(w_hi[b][:, :, :], w_raw[b][:, :, :], ACT.Copy).then_inc(w_hi_made[b], 1)

                def square(i):
                    act.wait_ge(x_in[i % 2], 16 * (i // 2 + 1))
                    act.activation(squares, x_tok[i % 2], ACT.Square, accum_out=sum_sq[:, i:i + 1])\
                       .then_inc(squared, 1)
                    act.wait_ge(squared, i + 1)
                    act.activation(root[:, i:i + 1], sum_sq[:, i:i + 1], ACT.Sqrt, bias=eps[:, 0:1],
                                   scale=1.0 / D_MODEL).then_inc(rooted, 1)

                def read_product(kind, pair, b, tb, previous):
                    act.wait_ge(product[tb], pair * 2 + b + 1)
                    if kind in "qkv":
                        if tb == 0:
                            free_fm(act, pair, b, previous)
                        done = act.activation(fm[b][:, block_cols(tb)], mm[tb][:, :], ACT.Copy,
                                              scale=-HEAD_DIM ** -0.5 if kind == "q" else 1.0)
                        done.then_inc(read_out[tb], 1)
                    elif kind in "gz":
                        act.activation(half_tanh[:, block_cols(tb)], mm[tb][:, :], ACT.Tanh, scale=0.5)\
                           .then_inc(gate_tanh, 1)
                    else:
                        if tb == 0 and (b == 1 or previous in CONVOLVED):
                            act.wait_ge(conv_step, (before_pair(CONVOLVED, kind, pair) * 2 + b) * CONV_K)
                        if tb == 0 and kind == "x" and b == 0:
                            act.wait_ge(padded, 1)
                        lo = CONV_K - 1 + tb * BANK
                        act.activation(conv_in[:, lo:lo + BANK], mm[tb][:, :], ACT.Copy).then_inc(read_out[tb], 1)

                def mark_made(kind, pair, b):
                    if kind in "qkv":
                        act.wait_ge(read_out[TB - 1], pair * 2 + b + 1)
                        act.sem_inc(fm_made[b], 1)

                act.wait_ge(consts_made, 3)
                square(0)
                split_high(0, 0)
                for i in range(TT):
                    if i + 1 < TT:
                        square(i + 1)
                    for h in range(2):
                        act.wait_ge(u_turned, 2 * i + h + 1)
                        act.activation(u_hi[:, h * 4:h * 4 + 4, i * P:(i + 1) * P],
                                       turn[2 * (i % 2) + h][:, :].rearrange("p (k t) -> p k t", t=P),
                                       ACT.Copy).then_inc(u_hi_made, 1)
                    if i - 1 in EARLY:
                        read_product("q", 0, *EARLY[i - 1], None)
                    if i == 2:
                        split_high(0, 1)
                read_product("q", 0, 0, TB - 1, None)
                mark_made("q", 0, 0)
                split_high(1, 0)
                read_product("q", 0, 1, TB - 1, None)
                mark_made("q", 0, 1)

                def step(kind, pair, previous):
                    if is_first(pair):
                        return
                    for b in range(2):
                        split_high(*((pair, 1) if b == 0 else (pair + 1, 0)))
                        for tb in range(TB):
                            read_product(kind, pair, b, tb, previous)
                        mark_made(kind, pair, b)
                        if kind in CONVOLVED:
                            done = before_pair(CONVOLVED, kind, pair) * 2 + b + 1
                            act.wait_ge(conv_step, done * CONV_K)
                            act.activation(half_tanh[:, :], fm[b][:, :], ACT.Tanh).then_inc(conv_tanh, 1)

                segment_steps(act, step)
                act.wait_ge(fm_out[0], 16 * total_pairs(STORED))
                for tb in range(TB):
                    act.wait_ge(product[tb], FT + 1)
                    act.activation(fm[0][0:SSM_HEADS, block_cols(tb)], mm[tb][0:SSM_HEADS, :],
                                   ACT.Copy).then_inc(dt_made, 1)

            @block.vector
            def _(dve):
                def normalise(i):
                    dve.wait_ge(rooted, i + 1)
                    dve.reciprocal(inv_rms[:, i:i + 1], root[:, i:i + 1]).then_inc(inverted, 1)
                    dve.wait_ge(inverted, i + 1)
                    if i >= 2:
                        dve.wait_ge(u_turned, 2 * (i - 1))
                    dve.scalar_tensor_tensor(out=u_tok[i % 2], in0=x_tok[i % 2], scalar=inv_rms[:, i:i + 1],
                                             in1=w_row, op0=ALU.mult, op1=ALU.mult).then_inc(normed, 1)

                dve.wait_ge(w_row_in, 16)
                normalise(0)
                for i in range(TT):
                    if i + 1 < TT:
                        normalise(i + 1)
                    for h in range(2):
                        dve.wait_ge(u_hi_made, 2 * i + h + 1)
                        part = (slice(None), slice(h * 4, h * 4 + 4), slice(i * P, (i + 1) * P))
                        dve.tensor_tensor(u_lo[part], turn[2 * (i % 2) + h][:, :].rearrange("p (k t) -> p k t", t=P),
                                          u_hi[part].bitcast(F32), ALU.subtract).then_inc(u_lo_made, 1)
                dve.wait_ge(normed, TT)
                dve.memset(conv_in[:, 0:CONV_K - 1], 0.0).then_inc(padded, 1)
                dve.wait_ge(taps_turned, 1)
                dve.tensor_scalar(taps[:, :], turn[0][:, 0:(CONV_K + 1) * n_conv], 0.5, None, ALU.mult)\
                   .then_inc(taps_halved, 1)
                dve.wait_ge(taps_halved, 1)

                def gate(kind, pair, b, previous):
                    for tb in range(TB):
                        dve.wait_ge(gate_tanh, (before_pair("gz", kind, pair) * 2 + b) * TB + tb + 1)
                        if tb == 0:
                            free_fm(dve, pair, b, previous)
                        dve.scalar_tensor_tensor(out=fm[b][:, block_cols(tb)], in0=half_tanh[:, block_cols(tb)],
                                                 scalar=1.0, in1=mm[tb][:, :], op0=ALU.add, op1=ALU.mult)\
                           .then_inc(read_out[tb], 1)
                    dve.wait_ge(read_out[TB - 1], pair * 2 + b + 1)
                    dve.sem_inc(fm_made[b], 1)

                def convolve(kind, pair, b, previous):
                    n = before_pair(CONVOLVED, kind, pair) * 2 + b
                    dve.wait_ge(read_out[TB - 1], pair * 2 + b + 1)
                    free_fm(dve, pair, b, previous)

                    def tap(j):
                        return taps[:, bass.ds(n + j * n_conv, 1)]

                    dve.tensor_scalar(fm[b][:, :], conv_in[:, 0:SEQ], tap(0), tap(CONV_K), ALU.mult, ALU.add)\
                       .then_inc(conv_step, 1)
                    for j in range(1, CONV_K):
                        dve.wait_ge(conv_step, n * CONV_K + j)
                        dve.scalar_tensor_tensor(out=fm[b][:, :], in0=conv_in[:, j:j + SEQ], scalar=tap(j),
                                                 in1=fm[b][:, :], op0=ALU.mult, op1=ALU.add).then_inc(conv_step, 1)
                    dve.wait_ge(conv_tanh, n + 1)
                    dve.scalar_tensor_tensor(out=fm[b][:, :], in0=half_tanh[:, :], scalar=1.0, in1=fm[b][:, :],
                                             op0=ALU.add, op1=ALU.mult).then_inc(fm_made[b], 1)

                def collect_turned(kind, pair, b):
                    n = turn_index(kind, pair, b)
                    for q in range(TB):
                        dve.wait_ge(turned, n * TB + q + 1)
                        if q == 0 and not (isinstance(n, int) and n == 0):
                            dve.wait_ge(tok_out, n * 16)
                        dve.tensor_copy(tok[:, q * 4:q * 4 + 4, :].rearrange("p a b -> p (a b)"), turn[q][:, :])\
                           .then_inc(tok_made, 1)

                def step(kind, pair, previous):
                    for b in range(2):
                        if kind in "gz":
                            gate(kind, pair, b, previous)
                        for k, r, bb in turned_in(kind, pair, previous):
                            if bb == 1 - b:
                                collect_turned(k, r, bb)
                        if kind in CONVOLVED:
                            convolve(kind, pair, b, previous)

                segment_steps(dve, step)

            @block.tensor
            def _(pe):
                def multiply(pair, b, tb):
                    t = pair * 2 + b
                    if tb == 0:
                        pe.wait_ge(w_lo_made[b], pair + 1)
                    if not (is_first(pair) and b == 0):
                        pe.wait_ge(read_out[tb], t)
                    for k in range(KT):
                        pe.matmul(mm[tb][:, :], w_hi[b][:, k, :], u_hi[:, k, block_cols(tb)], start=(k == 0), stop=False)
                        pe.matmul(mm[tb][:, :], w_hi[b][:, k, :], u_lo[:, k, block_cols(tb)], start=False, stop=False)
                        last = pe.matmul(mm[tb][:, :], w_lo[b][:, k, :], u_hi[:, k, block_cols(tb)],
                                         start=False, stop=(k == KT - 1))
                    last.then_inc(product[tb], 1)

                def turn_tile(kind, pair, b):
                    n = turn_index(kind, pair, b)
                    pe.wait_ge(fm_made[b], pair + 1)
                    for q in range(TB):
                        if not (isinstance(n, int) and n == 0):
                            pe.wait_ge(tok_made, (n - 1) * TB + q + 1)
                        for i in range(4):
                            tt = 4 * q + i
                            last = pe.transpose(turn[q][:, i * P:(i + 1) * P], fm[b][:, tt * P:(tt + 1) * P],
                                                ident[:, :])
                        last.then_inc(turned, 1)

                pe.wait_ge(consts_made, 3)
                for i in range(TT):
                    pe.wait_ge(normed, i + 1)
                    for h in range(2):
                        if i >= 2:
                            pe.wait_ge(u_lo_made, 2 * (i - 2) + h + 1)
                        for k in range(4):
                            last = pe.transpose(turn[2 * (i % 2) + h][:, k * P:(k + 1) * P],
                                                u_tok[i % 2][:, (h * 4 + k) * P:(h * 4 + k + 1) * P], ident[:, :])
                        last.then_inc(u_turned, 1)
                    if i in EARLY:
                        b, tb = EARLY[i]
                        pe.wait_ge(u_lo_made, 2 * (tb + 1) * TB)
                        multiply(0, b, tb)
                pe.wait_ge(u_lo_made, 2 * TT)
                for b in range(2):
                    multiply(0, b, TB - 1)
                pe.wait_ge(taps_in, 32)
                rows = (CONV_K + 1) * n_conv
                pe.transpose(turn[0][:, 0:rows], tap_rows[:, :], ident[0:rows, 0:rows]).then_inc(taps_turned, 1)

                def step(kind, pair, previous):
                    for b in range(2):
                        if not is_first(pair):
                            for tb in range(TB):
                                multiply(pair, b, tb)
                        for k, r, bb in turned_in(kind, pair, previous):
                            if bb == 1 - b:
                                if kind == "v" and isinstance(pair, int):
                                    pe.wait_ge(taps_halved, 1)
                                turn_tile(k, r, bb)

                segment_steps(pe, step)
                for tb in range(TB):
                    multiply(PAIRS, 0, tb)


CLASSES = 4
CLASS_LEN = SEQ // CLASSES
CLASS_BLOCKS = CLASS_LEN // P
SPAN = 128
UNITS = CLASSES * CLASS_BLOCKS + TT
CLASS_UNITS = CLASSES * CLASS_BLOCKS
GROUP = 8
WIDE = HEAD_DIM + 2


def attend(nc, dram, dt_bias, a_log, cum_tok, dt_tok):
    with ExitStack() as ctx:
        def sb(name, shape, dt=F32):
            return ctx.enter_context(nc.sbuf_tensor(name, shape, dt))

        def sem(name):
            return ctx.enter_context(nc.semaphore(name))

        S_BANKS, RING = 3, 4
        ident = sb("ident_b", [P, P])
        near_mask = sb("near_mask", [P, 2 * P])
        class_mask = sb("class_mask", [P, CLASS_LEN])
        raw = {x: sb(f"raw_{x}", [P, SEQ]) for x in "qk"}
        q_parts = [sb(f"q_parts{b}", [P, SEQ], F32R) for b in range(2)]
        k_high = [sb(f"k_high{b}", [P, SEQ], F32R) for b in range(2)]
        k_rest = [sb(f"k_rest{b}", [P, SEQ], F32R) for b in range(2)]
        g = sb("g", [P, SEQ])
        v_nat = [sb(f"v_nat{b}", [P, TT, HEAD_DIM]) for b in range(2)]
        v_cls = [sb(f"v_cls{b}", [P, CLASS_UNITS, HEAD_DIM]) for b in range(2)]
        masked = [sb(f"masked{r}", [P, BANK]) for r in range(RING)]
        probs = [sb(f"probs{r}", [P, BANK]) for r in range(RING)]
        probs_t = [sb(f"probs_t{r}", [P, BANK]) for r in range(RING)]
        dist, rem = masked[0][:, :].bitcast(I32), masked[1][:, :].bitcast(I32)
        count, near = masked[2], masked[3]
        cls_out = [sb(f"cls_out{b}", [P, CLASS_UNITS, WIDE]) for b in range(2)]
        cls_nat = [sb(f"cls_nat{b}", [P, TT, WIDE]) for b in range(2)]
        nat_out = [sb(f"nat_out{b}", [P, TT, HEAD_DIM]) for b in range(2)]
        nat_min = [sb(f"nat_min{b}", [P, TT]) for b in range(2)]
        nat_sum = [sb(f"nat_sum{b}", [P, TT]) for b in range(2)]
        both_min = sb("both_min", [P, TT])
        drop = sb("drop", [P, 2, TT])
        weight = sb("weight", [P, 2, TT])
        part_sum = sb("part_sum", [P, 2, TT])
        denom = sb("denom", [P, TT])
        inv_denom = sb("inv_denom", [P, TT])
        scale = sb("scale", [P, 2, TT])
        part_a = sb("part_a", [P, TT, HEAD_DIM])
        part_b = sb("part_b", [P, TT, HEAD_DIM])
        merged = sb("merged", [P, TT, 2, HEAD_DIM])
        gated = sb("gated", [P, SEQ])
        SEGS = P // SSM_HEADS
        SEG_LEN = SEQ // SEGS
        rooms = [room[:, :, :].rearrange("p a b -> p (a b)")[:, i * SEG_LEN:(i + 1) * SEG_LEN]
                 for room in (part_a, part_b) for i in range(4)]
        dt_raw, size, expd, one_plus, log1, gap, is_tiny, keep = rooms
        dt, cum = (merged[:, 0:TT // 2, :, :].rearrange("p a b c -> p (a b c)")[:, i * SEG_LEN:(i + 1) * SEG_LEN]
                   for i in range(2))
        by_segment = "h (s j) -> s h j"
        dt_cols = sb("dt_cols", [P, 3])

        ps_s = [ctx.enter_context(nc.psum_tensor(f"ps_s{i}", [P, BANK], F32)) for i in range(S_BANKS)]
        ps_t = [ctx.enter_context(nc.psum_tensor(f"ps_t{i}", [P, BANK], F32)) for i in range(2)]
        ps_o = [ctx.enter_context(nc.psum_tensor(f"ps_o{i}", [P, BANK], F32)) for i in range(2)]
        ps_x = ctx.enter_context(nc.psum_tensor("ps_x", [P, BANK], F32))

        made = sem("made")
        masks_made = sem("masks_made")
        raw_in = {x: sem(f"{x}_in") for x in "qk"}
        high_made = {x: sem(f"{x}_high_made") for x in "qk"}
        split = {x: sem(f"{x}_split") for x in "qk"}
        v_in = [sem(f"v_in{b}") for b in range(2)]
        g_in = sem("g_in")
        scored = sem("scored")
        masked_made = sem("masked_made")
        exped = sem("exped")
        probs_turned = sem("probs_turned")
        probs_t_made = [sem(f"probs_t_made{i}") for i in range(2)]
        weighed = sem("weighed")
        group_out = sem("group_out")
        relaid = sem("relaid")
        gate_turned = sem("gate_turned")
        x_read = sem("x_read")
        merge_step = sem("merge_step")
        weights_made = sem("weights_made")
        scales_made = sem("scales_made")
        merge_part = sem("merge_part")
        stored = sem("stored")
        last_out = sem("last_out")
        dve_waited = sem("dve_waited")
        dt_in = sem("dt_in")
        dt_step = sem("dt_step")
        dt_exped = sem("dt_exped")
        dt_logged = sem("dt_logged")
        cum_made = sem("cum_made")
        tok_turned = sem("tok_turned")

        def wait(eng, s, value):
            if not isinstance(value, int) or value > 0:
                eng.wait_ge(s, value)

        class Unit:

            def __init__(self, p):
                self.b, self.s = divmod(p, UNITS)
                self.group = self.s // GROUP
                if self.s < CLASS_UNITS:
                    n, c = divmod(self.s, CLASSES)
                    self.blocks = n + 1
                    self.q_cols = slice(n * BANK + c, (n + 1) * BANK, CLASSES)
                    self.k_cols = slice(c, self.blocks * BANK, CLASSES)
                    self.mask = class_mask[:, CLASS_LEN - self.blocks * P:]
                    self.v = [v_cls[self.b][:, c * CLASS_BLOCKS + j, :] for j in range(self.blocks)]
                    self.min = cls_out[self.b][:, self.s, HEAD_DIM + 1:HEAD_DIM + 2]
                    self.sum = cls_out[self.b][:, self.s, HEAD_DIM:HEAD_DIM + 1]
                else:
                    n = self.s - CLASS_UNITS
                    first = max(n - 1, 0)
                    self.blocks = n + 1 - first
                    self.q_cols = slice(n * P, (n + 1) * P)
                    self.k_cols = slice(first * P, (n + 1) * P)
                    self.mask = near_mask[:, 2 * P - self.blocks * P:]
                    self.v = [v_nat[self.b][:, j, :] for j in range(first, n + 1)]
                    self.min = nat_min[self.b][:, n:n + 1]
                    self.sum = nat_sum[self.b][:, n:n + 1]
                self.width = self.blocks * P

        STEPS = 2 * UNITS
        unit = [Unit(p) for p in range(STEPS)]
        GATE_STEP = {16: 0, 20: 1, 24: 2, 28: 3}
        MERGE_STEP = 3
        DT_TURN_STEP = 16
        HIGH_STEPS = {5 + 2 * i: (x, i % 4) for i, x in enumerate("qqqqkkkk")}

        def loop_pairs(eng, body):
            body(0)
            with eng.Fori(1, HEADS // 2 - 1) as pair:
                body(pair)
            body(HEADS // 2 - 1)

        def is_int(x, value):
            return isinstance(x, int) and x == value

        def is_first(pair):
            return is_int(pair, 0)

        def bank_user(p):
            return next(u for u in range(p - 1, p - 2 * S_BANKS, -1) if u % STEPS % S_BANKS == p % S_BANKS)

        def has_next(pair, b):
            return not is_int(pair * 2 + b, HEADS - 1)

        def ahead(do, pair, p, n):
            if p + n < STEPS:
                do(pair, p + n)
            elif has_next(pair, 1):
                do(pair + 1, p + n - STEPS)

        def behind(do, pair, p, n):
            if p >= n:
                do(pair, p - n)
            elif not is_first(pair):
                do(pair - 1, p - n + STEPS)

        def copy_probs(eng, pair, p, copy):
            u, base = unit[p], pair * STEPS
            eng.wait_ge(probs_turned, base + p + 1)
            wait(eng, weighed, base + p - RING + 1)
            copy(probs_t[p % RING][:, 0:u.width], ps_t[p % 2][:, 0:u.width]).then_inc(probs_t_made[p % 2], 1)

        def high_of(x, b, n):
            cols = slice(n * BANK, (n + 1) * BANK)
            return (q_parts if x == "q" else k_high)[b][:, cols], raw[x][:, cols]

        def take_rest(eng, x, b):
            if x == "q":
                rest = q_parts[b][HEAD_DIM:P, :]
                ins = eng.tensor_tensor(rest, raw[x][HEAD_DIM:P, :], rest.bitcast(F32), ALU.subtract)
            else:
                ins = eng.tensor_tensor(k_rest[b][:, :], raw[x][:, :], k_high[b][:, :].bitcast(F32), ALU.subtract)
            ins.then_inc(split[x], 1)

        def merge(eng, head, b):
            eng.wait_ge(scales_made, head + 1)
            wait(eng, merge_part, head * 3)
            for j, (dst, src) in enumerate(((part_a, nat_out[b][:, :, :]), (part_b, cls_nat[b][:, :, 0:HEAD_DIM]))):
                eng.tensor_tensor(dst[:, :, :], src, scale[:, j, :].unsqueeze(2).broadcast_to([P, TT, HEAD_DIM]),
                                  ALU.mult).then_inc(merge_part, 1)
            eng.wait_ge(merge_part, head * 3 + 2)
            if b == 0:
                wait(eng, gate_turned, head * (TB // 2))
            eng.tensor_tensor(merged[:, :, b, :], part_a[:, :, :], part_b[:, :, :], ALU.add).then_inc(merge_part, 1)

        last_banks = [ps_x] + ps_s

        with nc.Block() as block:
            @block.sync
            def _(sp):
                feat, tok = dram["feat"], dram["tok"]
                v_by_class = tok.rearrange("(n i c) f -> c i n f", n=CLASS_BLOCKS, c=CLASSES)
                v_natural = tok.rearrange("(n i) f -> i n f", i=P)

                def load_qk(head):
                    for x, at in (("q", 0), ("k", D_ATTN)):
                        wait(sp, split[x], head)
                        for rows in (slice(0, HEAD_DIM), slice(HEAD_DIM, P)):
                            sp.dma_start(raw[x][rows, :], feat[bass.ds(head * HEAD_DIM + at, HEAD_DIM), :])\
                              .then_inc(raw_in[x], 16)

                def relayout(head, b):
                    sp.wait_ge(group_out, head * (UNITS // GROUP) + CLASS_UNITS // GROUP)
                    rows = P // CLASSES
                    for c in range(CLASSES):
                        for j in range(CLASSES):
                            sp.dma_start(cls_nat[b][c:P:CLASSES, j:TT:CLASSES, :],
                                         cls_out[b][j * rows:(j + 1) * rows, c:CLASS_UNITS:CLASSES, :])\
                              .then_inc(relaid, 16)

                def load_head(head, b, is_last=False):
                    wait(sp, weighed, (head - 1) * UNITS)
                    cols = bass.ds(head * HEAD_DIM + V_COL, HEAD_DIM)
                    for c in range(CLASSES):
                        sp.dma_start(v_cls[b][:, c * CLASS_BLOCKS:(c + 1) * CLASS_BLOCKS, :], v_by_class[c][:, :, cols])\
                          .then_inc(v_in[b], 16)
                    sp.dma_start(v_nat[b][:, :, :], v_natural[:, :, cols]).then_inc(v_in[b], 16)
                    if not is_int(head, 0):
                        relayout(head - 1, 1 - b)
                    if not is_last:
                        load_qk(head + 1)
                    if b == 1:
                        wait(sp, x_read, (head - 1) * (TB // 2) + 1)
                        sp.dma_start(g[:, :], feat[bass.ds((head - 1) * HEAD_DIM + G_COL, P), :]).then_inc(g_in, 16)

                sp.dma_start(dt_raw, dram["dt"].rearrange(by_segment, s=SEGS)).then_inc(dt_in, 16)
                for j, src in enumerate((dt_bias, a_log)):
                    sp.dma_start(dt_cols[:, j:j + 1], src.rearrange("a h -> h a").unsqueeze(0)
                                 .broadcast_to([SEGS, SSM_HEADS, 1]), allow_slow_non_contiguous=True).then_inc(dt_in, 16)
                load_qk(0)
                load_head(0, 0)
                load_head(1, 1)
                with sp.Fori(1, HEADS // 2 - 1) as pair:
                    load_head(pair * 2, 0)
                    load_head(pair * 2 + 1, 1)
                load_head(HEADS - 2, 0)
                load_head(HEADS - 1, 1, is_last=True)
                sp.wait_ge(split["k"], HEADS)
                relayout(HEADS - 1, 1)
                for n in range(TB):
                    sp.wait_ge(x_read, (HEADS // 2 - 1) * TB + n + 2)
                    cols = slice(n * BANK, (n + 1) * BANK)
                    sp.dma_start(dram["attn"][D_ATTN - P:D_ATTN, cols], gated[:, cols]).then_inc(last_out, 16)
                sp.wait_ge(last_out, 16 * TB)

            @block.gpsimd
            def _(pool):
                pool.memset(ident[:, :], 0.0).then_inc(made, 1)
                pool.memset(near_mask[:, :], 0.0).then_inc(made, 1)
                pool.iota(dist, pattern=[[-1, CLASS_LEN]], base=CLASS_LEN - P, channel_multiplier=1).then_inc(made, 1)
                pool.wait_ge(made, 3)
                pool.affine_select(out=ident[:, :], in_=ident[:, :], compare_op=ALU.not_equal, fill=1.0,
                                   base=0, pattern=[[-1, P]], channel_multiplier=1).then_inc(made, 1)
                pool.affine_select(out=near_mask[:, :], in_=near_mask[:, :], compare_op=ALU.is_ge, fill=BIG,
                                   base=0, pattern=[[1, 2 * P]], channel_multiplier=-1).then_inc(made, 1)
                pool.wait_ge(made, 5)
                pool.affine_select(out=near_mask[:, :], in_=near_mask[:, :], compare_op=ALU.is_ge, fill=BIG,
                                   base=SPAN, pattern=[[-1, 2 * P]], channel_multiplier=1).then_inc(made, 1)
                pool.wait_ge(masks_made, 7)
                pool.affine_select(out=class_mask[:, :], in_=class_mask[:, :], compare_op=ALU.is_ge, fill=BIG,
                                   base=CLASS_LEN - P, pattern=[[-1, CLASS_LEN]], channel_multiplier=1).then_inc(made, 1)

                def store(pair):
                    pool.wait_ge(x_read, (pair + 1) * TB + 1)
                    pool.dma_start(dram["attn"][bass.ds(pair * P, P), :], gated[:, :]).then_inc(stored, 16)

                def head_turn(head, b, has_before=True, has_next=True):
                    if has_before:
                        merge(pool, head - 1, 1 - b)
                    if has_next:
                        wait(pool, scored, head * UNITS)
                        if has_before:
                            pool.wait_ge(merge_part, head * 3)
                        for x in "qk":
                            pool.wait_ge(high_made[x], (head + 2) * TB)
                            take_rest(pool, x, 1 - b)
                            if x == "q":
                                pool.wait_ge(split[x], head + 2)

                head_turn(0, 0, has_before=False)
                pool.wait_ge(cum_made, 1)
                pool.dma_start(dram["cum"].rearrange(by_segment, s=SEGS), cum).then_inc(stored, 16)
                pool.wait_ge(stored, 16)
                pool.wait_ge(x_read, 1)
                head_turn(1, 1)
                with pool.Fori(1, HEADS // 2 - 1) as pair:
                    head_turn(pair * 2, 0)
                    store(pair - 1)
                    head_turn(pair * 2 + 1, 1)
                head_turn(HEADS - 2, 0)
                store(HEADS // 2 - 2)
                head_turn(HEADS - 1, 1, has_next=False)
                pool.wait_ge(stored, 16 * (HEADS // 2))

            @block.vector
            def _(dve):
                step = [0]

                def mask_op(ins):
                    step[0] += 1
                    ins.then_inc(masks_made, 1)
                    dve.wait_ge(masks_made, step[0])

                dt_done = [0]

                def dt_op(ins):
                    dt_done[0] += 1
                    ins.then_inc(dt_step, 1)
                    dve.wait_ge(dt_step, dt_done[0])

                dve.wait_ge(dt_in, 48)
                dt_op(dve.tensor_scalar(dt_raw, dt_raw, dt_cols[:, 0:1], None, ALU.add))
                dt_op(dve.scalar_tensor_tensor(out=size, in0=dt_raw, scalar=-1.0, in1=dt_raw, op0=ALU.mult, op1=ALU.max))
                dve.wait_ge(dt_exped, 2)
                dt_op(dve.tensor_scalar(one_plus, expd, 1.0, None, ALU.add))

                def take_ratio():
                    dt_op(dve.tensor_scalar(gap, one_plus, -1.0, None, ALU.add))
                    dt_op(dve.tensor_scalar(is_tiny, gap, 0.0, None, ALU.is_equal))
                    dt_op(dve.tensor_tensor(gap, gap, is_tiny, ALU.add))
                    dt_op(dve.reciprocal(gap, gap))
                    dt_op(dve.tensor_tensor(gap, gap, expd, ALU.mult))

                def take_softplus():
                    dve.wait_ge(dt_logged, 1)
                    dt_op(dve.tensor_tensor(gap, gap, log1, ALU.mult))
                    dt_op(dve.tensor_tensor(is_tiny, is_tiny, expd, ALU.mult))
                    dt_op(dve.tensor_tensor(gap, gap, is_tiny, ALU.add))
                    dt_op(dve.scalar_tensor_tensor(out=dt, in0=dt_raw, scalar=0.0, in1=gap, op0=ALU.max, op1=ALU.add))

                def cumulate():
                    dt_op(dve.tensor_scalar(size, dt, dt_cols[:, 2:3], -1.0, ALU.mult, ALU.mult))
                    dt_op(dve.memset(keep, 1.0))
                    dt_op(dve.memset(keep.rearrange("p (a b) -> p a b", b=CHUNK)[:, :, 0:1], 0.0))
                    dve.tensor_tensor_scan(cum, keep, size, 0.0, ALU.mult, ALU.add).then_inc(cum_made, 1)

                def keep_tokens():
                    dve.wait_ge(tok_turned, 1)
                    for j, dst in enumerate((cum_tok, dt_tok)):
                        done = dve.tensor_copy(dst[:, :, :].rearrange("p (s a) h -> p a s h", a=2),
                                        ps_x[:, j * 2 * P:(j + 1) * 2 * P]
                                        .rearrange("p (a s h) -> p a s h", a=2, h=SSM_HEADS))
                    done.then_inc(x_read, 1)

                dve.wait_ge(made, 3)
                mask_op(dve.tensor_scalar(rem, dist, CLASSES - 1, None, ALU.bitwise_and))
                mask_op(dve.tensor_scalar(count[:, :], rem, 0, None, ALU.is_equal))
                mask_op(dve.tensor_scalar(near[:, :], dist, SPAN, None, ALU.is_le))
                mask_op(dve.tensor_tensor(count[:, :], count[:, :], near[:, :], ALU.add))
                mask_op(dve.tensor_scalar(near[:, :], count[:, :], 0.0, BIG, ALU.is_equal, ALU.mult))
                mask_op(dve.tensor_scalar(class_mask[:, :], count[:, :], 2.0, -LN2, ALU.is_equal, ALU.mult))
                mask_op(dve.tensor_tensor(class_mask[:, :], class_mask[:, :], near[:, :], ALU.add))
                dve.wait_ge(made, 7)
                for x in "qk":
                    dve.wait_ge(high_made[x], TB)
                    take_rest(dve, x, 0)

                def mask(pair, p):
                    u, base = unit[p], pair * STEPS
                    dve.wait_ge(scored, base + p + 1)
                    wait(dve, exped, base + p - RING + 1)
                    if u.s == 0:
                        wait(dve, scales_made, pair * 2 + u.b - 1)
                    dve.sem_inc(dve_waited, 1)
                    dve.tensor_tensor_reduce(out=masked[p % RING][:, 0:u.width], in0=ps_s[p % S_BANKS][:, 0:u.width],
                                             in1=u.mask, scale=1.0, scalar=3e38, op0=ALU.add, op1=ALU.min,
                                             accum_out=u.min).then_inc(masked_made, 1)

                def merge_drops(head, b):
                    mins = [nat_min[b][:, :], cls_nat[b][:, :, HEAD_DIM + 1]]
                    at = head * 9
                    dve.wait_ge(relaid, (head + 1) * CLASSES * CLASSES * 16)
                    dve.wait_ge(group_out, head * 4 + 4)
                    dve.wait_ge(exped, head * UNITS + UNITS)
                    dve.tensor_tensor(both_min[:, :], mins[0], mins[1], ALU.min).then_inc(merge_step, 1)
                    dve.wait_ge(merge_step, at + 1)
                    for j in range(2):
                        dve.tensor_tensor(drop[:, j, :], mins[j], both_min[:, :], ALU.subtract).then_inc(merge_step, 1)

                def merge_scales(head, b):
                    sums = [nat_sum[b][:, :], cls_nat[b][:, :, HEAD_DIM]]
                    at = head * 9
                    dve.wait_ge(weights_made, head + 1)
                    for j in range(2):
                        dve.tensor_tensor(part_sum[:, j, :], sums[j], weight[:, j, :], ALU.mult).then_inc(merge_step, 1)
                    dve.wait_ge(merge_step, at + 5)
                    dve.tensor_tensor(denom[:, :], part_sum[:, 0, :], part_sum[:, 1, :], ALU.add).then_inc(merge_step, 1)
                    dve.wait_ge(merge_step, at + 6)
                    dve.reciprocal(inv_denom[:, :], denom[:, :]).then_inc(merge_step, 1)
                    dve.wait_ge(merge_step, at + 7)
                    wait(dve, merge_part, head * 3)
                    dve.tensor_tensor(scale[:, 0, :], weight[:, 0, :], inv_denom[:, :], ALU.mult).then_inc(merge_step, 1)
                    dve.tensor_tensor(scale[:, 1, :], weight[:, 1, :], inv_denom[:, :], ALU.mult).then_inc(merge_step, 1)
                    dve.wait_ge(merge_step, at + 9)
                    dve.sem_inc(scales_made, 1)

                def gate_read(n, pair, bank=ps_x):
                    dve.wait_ge(gate_turned, pair * TB + n + 1)
                    if n == 0:
                        dve.wait_ge(g_in, (pair + 1) * 16)
                        dve.wait_ge(stored, (pair + 1) * 16)
                    cols = slice(n * BANK, (n + 1) * BANK)
                    dve.scalar_tensor_tensor(out=gated[:, cols], in0=bank[:, :], scalar=0.5, in1=g[:, cols],
                                             op0=ALU.mult, op1=ALU.mult).then_inc(x_read, 1)

                def copy_most(pair, p):
                    copy_probs(dve, pair, p, lambda o, i: dve.tensor_copy(o, i))

                def side(pair, p):
                    b, s = divmod(p, UNITS)
                    if is_first(pair) and b == 0:
                        if s == 4:
                            take_ratio()
                        if s == 8:
                            take_softplus()
                        if s == 12:
                            cumulate()
                        if s == DT_TURN_STEP + 2:
                            keep_tokens()
                        return
                    if s == MERGE_STEP:
                        merge_drops(pair * 2 + b - 1, 1 - b)
                    if s == MERGE_STEP + 2:
                        merge_scales(pair * 2 + b - 1, 1 - b)
                    if b == 0 and s - 1 in GATE_STEP:
                        gate_read(GATE_STEP[s - 1], pair - 1)

                def body(pair):
                    if is_first(pair):
                        mask(pair, 0)
                        mask(pair, 1)
                        mask(pair, 2)
                    for p in range(STEPS):
                        ahead(mask, pair, p, 3)
                        if p % 4 != 2:
                            copy_most(pair, p)
                        side(pair, p)

                loop_pairs(dve, body)
                merge_drops(HEADS - 1, 1)
                merge_scales(HEADS - 1, 1)
                merge(dve, HEADS - 1, 1)
                for n in range(4):
                    gate_read(n, HEADS // 2 - 1, last_banks[n])

            @block.scalar
            def _(act):
                def take_high(x, b, n, head):
                    if n == 0:
                        act.wait_ge(raw_in[x], (head + 1) * 32)
                        wait(act, scored, (head - 1) * UNITS)
                    dst, src = high_of(x, b, n)
                    act.activation(dst, src, ACT.Copy).then_inc(high_made[x], 1)

                act.wait_ge(dt_in, 48)
                act.activation(dt_cols[:, 2:3], dt_cols[:, 1:2], ACT.Exp).then_inc(dt_exped, 1)
                act.wait_ge(dt_step, 2)
                act.activation(expd, size, ACT.Exp, scale=-1.0).then_inc(dt_exped, 1)
                act.wait_ge(dt_step, 3)
                act.activation(log1, one_plus, ACT.Ln).then_inc(dt_logged, 1)

                for x in "qk":
                    for n in range(TB):
                        take_high(x, 0, n, 0)

                def exponentiate(pair, p):
                    u, base = unit[p], pair * STEPS
                    if u.s == 0:
                        wait(act, scales_made, pair * 2 + u.b - 1)
                    act.wait_ge(masked_made, base + p + 1)
                    wait(act, probs_turned, base + p - RING + 1)
                    act.activation(probs[p % RING][:, 0:u.width], masked[p % RING][:, 0:u.width], ACT.Exp,
                                   bias=u.min, scale=-1.0, accum_out=u.sum).then_inc(exped, 1)

                def group_read(pair, p):
                    u = unit[p]
                    act.wait_ge(weighed, pair * STEPS + p + 1)
                    at = (u.group % 2) * GROUP
                    dst = (cls_out[u.b][:, at:at + GROUP, 0:HEAD_DIM] if u.s < CLASS_UNITS
                           else nat_out[u.b][:, at:at + GROUP, :])
                    if u.group == 2:
                        wait(act, merge_part, (pair * 2 + u.b - 1) * 3)
                    act.activation(dst, ps_o[u.group % 2][:, :].rearrange("p (u f) -> p u f", f=HEAD_DIM), ACT.Copy)\
                       .then_inc(group_out, 1)

                def weights(head):
                    act.wait_ge(merge_step, head * 9 + 3)
                    act.activation(weight[:, :, :], drop[:, :, :], ACT.Exp, scale=-1.0).then_inc(weights_made, 1)

                def side(pair, p):
                    b, s = divmod(p, UNITS)
                    if (p - 2) % GROUP == 0:
                        behind(group_read, pair, p, 3)
                    if s == MERGE_STEP + 1 and not (is_first(pair) and b == 0):
                        weights(pair * 2 + b - 1)
                    if s in HIGH_STEPS and has_next(pair, b):
                        x, n = HIGH_STEPS[s]
                        take_high(x, 1 - b, n, pair * 2 + b + 1)

                def body(pair):
                    if is_first(pair):
                        exponentiate(pair, 0)
                    for p in range(STEPS):
                        ahead(exponentiate, pair, p, 1)
                        if p % 4 == 2:
                            copy_probs(act, pair, p, lambda o, i: act.activation(o, i, ACT.Copy))
                        side(pair, p)

                loop_pairs(act, body)
                group_read(HEADS // 2 - 1, STEPS - 1)
                weights(HEADS - 1)

            @block.tensor
            def _(pe):
                def score(pair, p):
                    u, base = unit[p], pair * STEPS
                    if u.s == 0:
                        pe.wait_ge(split["q"], pair * 2 + u.b + 1)
                        pe.wait_ge(split["k"], pair * 2 + u.b + 1)
                    wait(pe, masked_made, base + bank_user(p) + 1)
                    bank = ps_s[p % S_BANKS][:, 0:u.width]
                    pe.matmul(bank, q_parts[u.b][:, u.q_cols], k_high[u.b][:, u.k_cols], start=True, stop=False)
                    pe.matmul(bank, q_parts[u.b][:, u.q_cols], k_rest[u.b][:, u.k_cols], start=False, stop=True)\
                      .then_inc(scored, 1)

                def turn_probs(pair, p):
                    u, base = unit[p], pair * STEPS
                    pe.wait_ge(exped, base + p + 1)
                    wait(pe, probs_t_made[p % 2], pair * (STEPS // 2) + p // 2)
                    for j in range(u.blocks):
                        last = pe.transpose(ps_t[p % 2][:, j * P:(j + 1) * P], probs[p % RING][:, j * P:(j + 1) * P],
                                            ident[:, :])
                    last.then_inc(probs_turned, 1)

                def weigh(pair, p):
                    u = unit[p]
                    if u.s == 0:
                        pe.wait_ge(v_in[u.b], (pair + 1) * (CLASSES + 1) * 16)
                    pe.wait_ge(probs_t_made[p % 2], pair * (STEPS // 2) + p // 2 + 1)
                    if u.s % GROUP == 0:
                        wait(pe, group_out, pair * (STEPS // GROUP) + p // GROUP - 1)
                    for j in range(u.blocks):
                        last = pe.matmul(ps_o[u.group % 2][:, (u.s % GROUP) * HEAD_DIM:(u.s % GROUP + 1) * HEAD_DIM],
                                         probs_t[p % RING][:, j * P:(j + 1) * P], u.v[j],
                                         start=(j == 0), stop=(j == u.blocks - 1))
                    last.then_inc(weighed, 1)

                def turn_merged(n, pair, bank=ps_x):
                    pe.wait_ge(merge_part, (pair + 1) * 2 * 3)
                    if bank is ps_x:
                        pe.wait_ge(x_read, pair * TB + n + 1)
                    for j in range(TT // TB):
                        last = pe.transpose(bank[:, j * P:(j + 1) * P],
                                            merged[:, n * 4 + j, :, :].rearrange("p b f -> p (b f)"), ident[:, :])
                    last.then_inc(gate_turned, 1)

                def turn_dt():
                    pe.wait_ge(cum_made, 1)
                    for j, src in enumerate((cum, dt)):
                        for a in range(2):
                            last = pe.transpose(ps_x[:, (2 * j + a) * P:(2 * j + a + 1) * P],
                                                src[:, a * P:(a + 1) * P], ident[:, :])
                    last.then_inc(tok_turned, 1)

                def side(pair, p):
                    b, s = divmod(p, UNITS)
                    if is_first(pair) and p == DT_TURN_STEP:
                        turn_dt()
                    if b == 0 and s in GATE_STEP and not is_first(pair):
                        turn_merged(GATE_STEP[s], pair - 1)

                def body(pair):
                    if is_first(pair):
                        for p in range(3):
                            score(pair, p)
                    for p in range(STEPS):
                        ahead(score, pair, p, 3)
                        turn_probs(pair, p)
                        behind(weigh, pair, p, 2)
                        side(pair, p)

                pe.wait_ge(made, 7)
                loop_pairs(pe, body)
                for p in range(STEPS - 2, STEPS):
                    weigh(HEADS // 2 - 1, p)
                pe.wait_ge(masked_made, HEADS * UNITS)
                for n in range(TB):
                    turn_merged(n, HEADS // 2 - 1, last_banks[n])


def scan_and_project(nc, dram, cum_tok, dt_tok, x, w_out, d_skip, ssm_norm_w, norm_post_w, out):
    with ExitStack() as ctx:
        def sb(name, shape, dt=F32):
            return ctx.enter_context(nc.sbuf_tensor(name, shape, dt))

        def sem(name):
            return ctx.enter_context(nc.semaphore(name))

        def ps(name):
            return ctx.enter_context(nc.psum_tensor(name, [P, BANK], F32))

        KO = 2 * D_MODEL // P
        KA = D_ATTN // P
        HD = SSM_HEADS * HEAD_DIM
        GW = HEADS_PER_GROUP * HEAD_DIM

        ident = sb("ident_c", [P, P])
        causal = sb("causal", [P, P])
        wo_hi = sb("wo_hi", [P, KO, D_MODEL], F32R)
        wo_lo = sb("wo_lo", [P, KO, D_MODEL], F32R)
        mix_hi = sb("mix_hi", [P, KO, P], F32R)
        mix_lo = sb("mix_lo", [P, KO, P], F32R)
        post_w = sb("post_w", [P, D_MODEL])
        norm_w = sb("norm_w", [P, KA])
        skip = sb("skip", [P, SSM_HEADS])
        cum_b = sb("cum_b", [P, SSM_HEADS, CHUNK])
        decay = sb("decay", [P, SSM_HEADS, CHUNK])
        xs = sb("xs", [P, SSM_HEADS, HEAD_DIM])
        x_dt = sb("x_dt", [P, SSM_HEADS, HEAD_DIM])
        y = sb("y", [P, SSM_HEADS, HEAD_DIM])
        z2 = sb("z2", [P, HD])
        b_tok = sb("b_tok", [P, SSM_GROUPS, D_STATE])
        bc_t = sb("bc_t", [P, 2 * SSM_GROUPS, CHUNK])
        state = sb("state", [P, SSM_HEADS, HEAD_DIM])
        attn_t = sb("attn_t", [P, KA, P])
        x_res = sb("x_res", [P, D_MODEL])
        o_tok = sb("o_tok", [P, D_MODEL])
        wo_room = sb("wo_room", [P, D_MODEL])
        cb = sb("cb", [P, SSM_GROUPS, CHUNK])
        small = sb("small", [P, 3, SSM_HEADS])
        grown = sb("grown", [P, 3, SSM_HEADS])
        ssq = sb("ssq", [P, 4])
        mean = sb("mean", [P, 4])
        rstd = sb("rstd", [P, 4])
        minus_half = sb("minus_half", [P, 4])
        wo_raw = [x_res[:, :], o_tok[:, :], post_w[:, :], wo_room[:, :]]
        ROOMS = len(wo_raw)
        PORTION = [range(i * KO // 4, (i + 1) * KO // 4) for i in range(4)]

        ps_cb = ps("ps_cb")
        ps_state = [ps("ps_state0"), ps("ps_state1")]
        ps_turn = ps_state
        ps_y = [ps("ps_y0"), ps("ps_y1")]
        ps_out = [ps("ps_out0"), ps("ps_out1")]

        names = ("made rows_in post_in wo_hi_made "
                 "wo_lo_made xs_in z_in b_in bc_in cum_in attn_in x_in "
                 "small_made grown_made seg_made seg_bounded decayed cb_done "
                 "cb_made weighed_made x_dt_made x_end_made skipped states_done off_done y_off_made state_faded "
                 "state_made y_skip diag_done y_diag_made y_gated y_squared y_rstd y_scaled y_turned mix_hi_made "
                 "mix_lo_made attn_hi_made attn_lo_made out_done out_squared out_rstd out_scaled out_added stored "
                 "mean_made root_made pool_waited").split()
        S = {n: sem("c_" + n) for n in names}
        wo_in = [sem(f"c_wo_in{b}") for b in range(ROOMS)]

        def wait(eng, name, value):
            if not isinstance(value, int) or value > 0:
                eng.wait_ge(S[name], value)

        def chunks(eng, body):
            for c in range(3):
                body(c)
            with eng.Fori(3, CHUNKS) as c:
                body(c)

        def is_zero(c):
            return isinstance(c, int) and c == 0

        def has(c):
            return not isinstance(c, int) or c >= 0

        group = [slice(g * GW, (g + 1) * GW) for g in range(SSM_GROUPS)]
        heads_of = [slice(g * HEADS_PER_GROUP, (g + 1) * HEADS_PER_GROUP) for g in range(SSM_GROUPS)]
        y_flat = y[:, :, :].rearrange("p h d -> p (h d)")

        def spread(ap, n):
            return ap.unsqueeze(2).broadcast_to([P, ap.shape[1], n])

        with nc.Block() as block:
            @block.sync
            def _(sp):
                def load_w_out(tiles):
                    for t in tiles:
                        if t >= ROOMS:
                            sp.wait_ge(S["wo_lo_made"], t - ROOMS + 1)
                        sp.dma_start(wo_raw[t % ROOMS], w_out[t * P:(t + 1) * P, :]).then_inc(wo_in[t % ROOMS], 16)

                def load(c):
                    tokens = bass.ds(c * CHUNK, CHUNK)
                    wait(sp, "seg_made", c)
                    wait(sp, "small_made", c)
                    sp.dma_start(cum_b[:, :, :], dram["cum"][:, tokens].unsqueeze(0).broadcast_to([P, SSM_HEADS, CHUNK]))\
                      .then_inc(S["cum_in"], 16)
                    wait(sp, "cb_done", c)
                    wait(sp, "off_done", c)
                    sp.dma_start(bc_t[:, :, :], dram["feat"][D_B0:D_B0 + 4 * P, :]
                                 .rearrange("(q n) t -> n q t", n=P)[:, :, tokens]).then_inc(S["bc_in"], 16)
                    if is_zero(c):
                        load_w_out(range(ROOMS))
                    wait(sp, "states_done", c)
                    sp.dma_start(b_tok[:, :, :].rearrange("p g n -> p (g n)"), dram["tok"][tokens, D_B0:D_B0 + 2 * P])\
                      .then_inc(S["b_in"], 16)
                    wait(sp, "y_skip", c)
                    sp.dma_start(xs[:, :, :].rearrange("p h d -> p (h d)"), dram["tok"][tokens, D_X0:D_X0 + D_SSM])\
                      .then_inc(S["xs_in"], 16)
                    wait(sp, "y_gated", c)
                    sp.dma_start(z2[:, :], dram["tok"][tokens, Z_COL:Z_COL + D_SSM]).then_inc(S["z_in"], 16)
                    wait(sp, "attn_lo_made", c)
                    sp.dma_start(attn_t[:, :, :], dram["attn"].rearrange("(k p) t -> p k t", p=P)[:, :, tokens])\
                      .then_inc(S["attn_in"], 16)
                    if is_zero(c):
                        sp.dma_start(skip[:, :], d_skip.broadcast_to([P, SSM_HEADS])).then_inc(S["rows_in"], 16)
                        sp.dma_start(norm_w[:, :], ssm_norm_w.rearrange("a (n p) -> p (a n)", p=P),
                                     allow_slow_non_contiguous=True).then_inc(S["rows_in"], 16)
                        load_w_out(range(ROOMS, KO))

                load(0)
                load(1)
                sp.wait_ge(S["wo_lo_made"], KO)
                sp.dma_start(post_w[:, :], norm_post_w.broadcast_to([P, D_MODEL])).then_inc(S["post_in"], 16)
                with sp.Fori(2, CHUNKS) as c:
                    load(c)

            @block.gpsimd
            def _(pool):
                pool.memset(ident[:, :], 0.0).then_inc(S["made"], 1)
                pool.memset(causal[:, :], 1.0).then_inc(S["made"], 1)
                pool.memset(minus_half[:, :], -0.5).then_inc(S["made"], 1)
                pool.memset(state[:, :, :], 0.0).then_inc(S["made"], 1)
                pool.wait_ge(S["made"], 4)
                pool.affine_select(out=ident[:, :], in_=ident[:, :], compare_op=ALU.not_equal, fill=1.0,
                                   base=0, pattern=[[-1, P]], channel_multiplier=1).then_inc(S["made"], 1)
                pool.affine_select(out=causal[:, :], in_=causal[:, :], compare_op=ALU.is_ge, fill=0.0,
                                   base=0, pattern=[[1, P]], channel_multiplier=-1).then_inc(S["made"], 1)

                def residual(c):
                    wait(pool, "out_added", c)
                    pool.dma_start(x_res[:, :], x[bass.ds(c * CHUNK, CHUNK), :]).then_inc(S["x_in"], 16)

                def store(c):
                    pool.wait_ge(S["out_added"], c + 1)
                    pool.dma_start(out[bass.ds(c * CHUNK, CHUNK), :], o_tok[:, :]).then_inc(S["stored"], 16)

                def finish_output(c):
                    pool.wait_ge(S["out_squared"], 2 * (c + 1))
                    pool.tensor_tensor(mean[:, 2:3], ssq[:, 2:3], ssq[:, 3:4], ALU.add).then_inc(S["root_made"], 1)
                    pool.wait_ge(S["root_made"], 2 * c + 1)
                    pool.sem_inc(S["pool_waited"], 1)
                    pool.tensor_scalar(mean[:, 3:4], mean[:, 2:3], 1.0 / D_MODEL, EPS, ALU.mult, ALU.add)\
                        .then_inc(S["root_made"], 1)
                    pool.wait_ge(S["root_made"], 2 * c + 2)
                    pool.tensor_tensor(rstd[:, 2:3], mean[:, 3:4], minus_half[:, 2:3], ALU.pow).then_inc(S["out_rstd"], 1)
                    pool.wait_ge(S["out_scaled"], 2 * (c + 1))
                    pool.wait_ge(S["x_in"], 16 * (c + 1))
                    pool.tensor_tensor(o_tok[:, :], o_tok[:, :], x_res[:, :], ALU.add).then_inc(S["out_added"], 1)

                def body(c):
                    pool.wait_ge(S["xs_in"], (c + 1) * 16)
                    wait(pool, "diag_done", c)
                    pool.tensor_tensor(x_dt[:, :, :], xs[:, :, :], spread(dt_of(c), HEAD_DIM), ALU.mult)\
                        .then_inc(S["x_dt_made"], 1)
                    pool.wait_ge(S["grown_made"], c + 1)
                    pool.wait_ge(S["x_dt_made"], c + 1)
                    wait(pool, "y_turned", c)
                    pool.tensor_tensor(y[:, :, :], x_dt[:, :, :], spread(grown[:, 1, :], HEAD_DIM), ALU.mult)\
                        .then_inc(S["x_end_made"], 1)
                    pool.wait_ge(S["off_done"], c + 1)
                    wait(pool, "state_made", c)
                    pool.tensor_tensor(state[:, :, :], state[:, :, :], spread(grown[:, 0, :], HEAD_DIM), ALU.mult)\
                        .then_inc(S["state_faded"], 1)
                    if is_zero(c):
                        pool.wait_ge(S["rows_in"], 32)
                    pool.tensor_tensor(xs[:, :, :], xs[:, :, :], spread(skip[:, :], HEAD_DIM), ALU.mult)\
                        .then_inc(S["skipped"], 1)
                    if has(c - 2):
                        finish_output(c - 2)
                        store(c - 2)
                        residual(c - 1)
                    pool.wait_ge(S["y_squared"], 2 * (c + 1))
                    pool.sem_inc(S["pool_waited"], 1)
                    pool.tensor_scalar(mean[:, 0:2], ssq[:, 0:2], 1.0 / GW, EPS, ALU.mult, ALU.add)\
                        .then_inc(S["mean_made"], 1)
                    pool.wait_ge(S["mean_made"], c + 1)
                    pool.tensor_tensor(rstd[:, 0:2], mean[:, 0:2], minus_half[:, 0:2], ALU.pow).then_inc(S["y_rstd"], 1)
                    wait(pool, "out_done", c * 2)
                    pool.wait_ge(S["attn_hi_made"], c + 1)
                    pool.tensor_tensor(mix_lo[:, 0:KA, :], attn_t[:, :, :], mix_hi[:, 0:KA, :].bitcast(F32),
                                       ALU.subtract).then_inc(S["attn_lo_made"], 1)
                    if is_zero(c):
                        pool.wait_ge(S["wo_lo_made"], KO)
                        residual(0)

                def dt_of(c):
                    return dt_tok[:, bass.ds(c, 1), :].rearrange("p a h -> p (a h)")

                chunks(pool, body)
                for c in (CHUNKS - 2, CHUNKS - 1):
                    finish_output(c)
                    store(c)
                    if c < CHUNKS - 1:
                        residual(c + 1)
                pool.wait_ge(S["stored"], 16 * CHUNKS)

            @block.vector
            def _(dve):
                def take_low(tiles):
                    for t in tiles:
                        raw = wo_raw[t % ROOMS]
                        dve.wait_ge(S["wo_hi_made"], t + 1)
                        if t < KA:
                            done = dve.tensor_tensor(wo_lo[:, t, :], raw, wo_hi[:, t, :].bitcast(F32), ALU.subtract)
                        else:
                            done = dve.scalar_tensor_tensor(out=wo_lo[:, t, :], in0=raw, scalar=norm_w[:, t - KA:t - KA + 1],
                                                            in1=wo_hi[:, t, :].bitcast(F32), op0=ALU.mult,
                                                            op1=ALU.subtract)
                        done.then_inc(S["wo_lo_made"], 1)

                def out_scale(c):
                    if is_zero(c):
                        dve.wait_ge(S["post_in"], 16)
                    dve.wait_ge(S["out_rstd"], c + 1)
                    for h in range(2):
                        half = slice(h * BANK, (h + 1) * BANK)
                        dve.scalar_tensor_tensor(out=o_tok[:, half], in0=o_tok[:, half], scalar=rstd[:, 2:3],
                                                 in1=post_w[:, half], op0=ALU.mult, op1=ALU.mult)\
                           .then_inc(S["out_scaled"], 1)

                def body(c):
                    cum_c = cum_tok[:, bass.ds(c, 1), :].rearrange("p a h -> p (a h)")
                    dve.wait_ge(S["cum_in"], (c + 1) * 16)
                    wait(dve, "grown_made", c)
                    last = cum_b[:, :, CHUNK - 1:CHUNK].rearrange("p h a -> p (h a)")
                    dve.tensor_copy(small[:, 0, :], last)
                    dve.tensor_tensor(small[:, 1, :], last, cum_c, ALU.subtract)
                    dve.tensor_copy(small[:, 2, :], cum_c).then_inc(S["small_made"], 1)
                    wait(dve, "diag_done", c)
                    dve.tensor_tensor(decay[:, :, :], cum_b[:, :, :], spread(cum_c, CHUNK), ALU.subtract)\
                       .then_inc(S["seg_made"], 1)
                    dve.wait_ge(S["seg_made"], c + 1)
                    dve.tensor_scalar(decay[:, :, :], decay[:, :, :], 0.0, None, ALU.min).then_inc(S["seg_bounded"], 1)
                    dve.wait_ge(S["cb_done"], c + 1)
                    dve.tensor_tensor(cb[:, :, :], ps_cb[:, 0:SSM_GROUPS * CHUNK].rearrange("p (g l) -> p g l", l=CHUNK),
                                      causal[:, :].unsqueeze(1).broadcast_to([P, SSM_GROUPS, CHUNK]), ALU.mult)\
                       .then_inc(S["cb_made"], 1)
                    if is_zero(c):
                        take_low(PORTION[0])
                    dve.wait_ge(S["decayed"], c + 1)
                    dve.wait_ge(S["cb_made"], c + 1)
                    for g in range(SSM_GROUPS):
                        dve.tensor_tensor(decay[:, heads_of[g], :], decay[:, heads_of[g], :],
                                          cb[:, g, :].unsqueeze(1).broadcast_to([P, HEADS_PER_GROUP, CHUNK]),
                                          ALU.mult).then_inc(S["weighed_made"], 1)
                    dve.wait_ge(S["off_done"], c + 1)
                    dve.wait_ge(S["states_done"], c + 1)
                    dve.wait_ge(S["grown_made"], c + 1)
                    for g in range(SSM_GROUPS):
                        dve.tensor_tensor(y[:, heads_of[g], :], ps_y[g][:, :].rearrange("p (h d) -> p h d", d=HEAD_DIM),
                                          spread(grown[:, 2, heads_of[g]], HEAD_DIM), ALU.mult).then_inc(S["y_off_made"], 1)
                    dve.wait_ge(S["state_faded"], c + 1)
                    for g in range(SSM_GROUPS):
                        st = state[:, heads_of[g], :].rearrange("p h d -> p (h d)")
                        done = dve.tensor_tensor(st, st, ps_state[g][:, :], ALU.add)
                    done.then_inc(S["state_made"], 1)
                    dve.wait_ge(S["skipped"], c + 1)
                    dve.wait_ge(S["y_off_made"], 2 * (c + 1))
                    dve.tensor_tensor(y[:, :, :], y[:, :, :], xs[:, :, :], ALU.add).then_inc(S["y_skip"], 1)
                    if is_zero(c):
                        take_low(PORTION[1])
                    if has(c - 2):
                        out_scale(c - 2)
                    dve.wait_ge(S["diag_done"], c + 1)
                    dve.wait_ge(S["y_skip"], c + 1)
                    for g in range(SSM_GROUPS):
                        done = dve.tensor_tensor(y_flat[:, group[g]], y_flat[:, group[g]], ps_y[g][:, :], ALU.add)
                    done.then_inc(S["y_diag_made"], 1)
                    dve.wait_ge(S["y_diag_made"], c + 1)
                    dve.wait_ge(S["z_in"], (c + 1) * 16)
                    dve.scalar_tensor_tensor(out=y_flat, in0=y_flat, scalar=0.5, in1=z2[:, :], op0=ALU.mult,
                                             op1=ALU.mult).then_inc(S["y_gated"], 1)
                    if is_zero(c):
                        take_low(PORTION[2])
                        take_low(PORTION[3])
                    for h in range(2):
                        dve.wait_ge(S["mix_hi_made"], 2 * c + h + 1)
                        at = slice(KA + 4 * h, KA + 4 * h + 4)
                        dve.tensor_tensor(mix_lo[:, at, :], ps_turn[h][:, :].rearrange("p (k t) -> p k t", t=P),
                                          mix_hi[:, at, :].bitcast(F32), ALU.subtract).then_inc(S["mix_lo_made"], 1)

                chunks(dve, body)
                out_scale(CHUNKS - 2)
                out_scale(CHUNKS - 1)

            @block.scalar
            def _(act):
                def take_high(tiles):
                    for t in tiles:
                        act.wait_ge(wo_in[t % ROOMS], 16 * (t // ROOMS + 1))
                        if t == KA:
                            act.wait_ge(S["rows_in"], 32)
                        act.activation(wo_hi[:, t, :], wo_raw[t % ROOMS], ACT.Copy,
                                       scale=1.0 if t < KA else norm_w[:, t - KA:t - KA + 1]).then_inc(S["wo_hi_made"], 1)

                def out_read(c, h):
                    act.wait_ge(S["out_done"], 2 * c + h + 1)
                    if h == 0:
                        wait(act, "stored", c * 16)
                    act.activation(o_tok[:, h * BANK:(h + 1) * BANK], ps_out[h][:, :], ACT.Copy)
                    act.activation(ps_out[h][:, :], ps_out[h][:, :], ACT.Square,
                                   accum_out=ssq[:, 2 + h:3 + h]).then_inc(S["out_squared"], 1)

                def body(c):
                    act.wait_ge(S["small_made"], c + 1)
                    wait(act, "state_faded", c)
                    act.activation(grown[:, :, :], small[:, :, :], ACT.Exp).then_inc(S["grown_made"], 1)
                    act.wait_ge(S["seg_bounded"], c + 1)
                    act.activation(decay[:, :, :], decay[:, :, :], ACT.Exp).then_inc(S["decayed"], 1)
                    if is_zero(c):
                        take_high(PORTION[0])
                        take_high(PORTION[1])
                    if has(c - 1):
                        out_read(c - 1, 0)
                    act.wait_ge(S["y_gated"], c + 1)
                    for g in range(SSM_GROUPS):
                        wait(act, "y_skip", c + 1)
                        act.activation(squares(g), y_flat[:, group[g]], ACT.Square, accum_out=ssq[:, g:g + 1])\
                           .then_inc(S["y_squared"], 1)
                    if is_zero(c):
                        take_high(PORTION[2])
                    act.wait_ge(S["y_rstd"], c + 1)
                    for g in range(SSM_GROUPS):
                        act.activation(y_flat[:, group[g]], y_flat[:, group[g]], ACT.Copy, scale=rstd[:, g:g + 1])\
                           .then_inc(S["y_scaled"], 1)
                    if is_zero(c):
                        take_high(PORTION[3])
                    act.wait_ge(S["attn_in"], (c + 1) * 16)
                    wait(act, "out_done", c * 2)
                    act.activation(mix_hi[:, 0:KA, :], attn_t[:, :, :], ACT.Copy).then_inc(S["attn_hi_made"], 1)
                    for h in range(2):
                        act.wait_ge(S["y_turned"], c + 1)
                        act.activation(mix_hi[:, KA + 4 * h:KA + 4 * h + 4, :],
                                       ps_turn[h][:, :].rearrange("p (k t) -> p k t", t=P), ACT.Copy)\
                           .then_inc(S["mix_hi_made"], 1)
                    if has(c - 1):
                        out_read(c - 1, 1)

                def squares(g):
                    return x_dt[:, heads_of[g], :].rearrange("p h d -> p (h d)")

                chunks(act, body)
                for h in range(2):
                    out_read(CHUNKS - 1, h)

            @block.tensor
            def _(pe):
                pe.wait_ge(S["made"], 6)
                def project(c, h, mixer):
                    if h == 0 and mixer == "attention":
                        if is_zero(c):
                            pe.wait_ge(S["wo_lo_made"], KO)
                        pe.wait_ge(S["attn_hi_made"], c + 1)
                    if h == 0 and mixer == "scan":
                        pe.wait_ge(S["mix_hi_made"], 2 * (c + 1))
                    if mixer == "attention":
                        wait(pe, "out_squared", 2 * (c - 1) + h + 1)
                    cols_h = slice(h * BANK, (h + 1) * BANK)
                    tiles = range(KA) if mixer == "attention" else range(KA, KO)
                    for kk in tiles:
                        pe.matmul(ps_out[h][:, :], mix_hi[:, kk, :], wo_hi[:, kk, cols_h], start=(kk == 0), stop=False)
                        pe.matmul(ps_out[h][:, :], mix_hi[:, kk, :], wo_lo[:, kk, cols_h], start=False, stop=False)
                    if h == 0:
                        if mixer == "attention":
                            pe.wait_ge(S["attn_lo_made"], c + 1)
                        else:
                            pe.wait_ge(S["mix_lo_made"], 2 * (c + 1))
                    for kk in tiles:
                        last = pe.matmul(ps_out[h][:, :], mix_lo[:, kk, :], wo_hi[:, kk, cols_h],
                                         start=False, stop=(kk == KO - 1))
                    if mixer == "scan":
                        last.then_inc(S["out_done"], 1)

                def body(c):
                    pe.wait_ge(S["bc_in"], (c + 1) * 16)
                    wait(pe, "cb_made", c)
                    for g in range(SSM_GROUPS):
                        last = pe.matmul(ps_cb[:, g * CHUNK:(g + 1) * CHUNK], bc_t[:, g, :], bc_t[:, SSM_GROUPS + g, :],
                                         start=True, stop=True)
                    last.then_inc(S["cb_done"], 1)
                    wait(pe, "state_made", c)
                    wait(pe, "y_diag_made", c)
                    for g in range(SSM_GROUPS):
                        last = pe.matmul(ps_y[g][:, :], bc_t[:, SSM_GROUPS + g, :],
                                         state[:, heads_of[g], :].rearrange("p h d -> p (h d)"), start=True, stop=True)
                    last.then_inc(S["off_done"], 1)
                    if has(c - 1):
                        project(c - 1, 0, "attention")
                    pe.wait_ge(S["b_in"], (c + 1) * 16)
                    pe.wait_ge(S["x_end_made"], c + 1)
                    wait(pe, "mix_lo_made", 2 * c)
                    for g in range(SSM_GROUPS):
                        last = pe.matmul(ps_state[g][:, :], b_tok[:, g, :],
                                         y[:, heads_of[g], :].rearrange("p h d -> p (h d)"), start=True, stop=True)
                    last.then_inc(S["states_done"], 1)
                    if has(c - 1):
                        project(c - 1, 0, "scan")
                    pe.wait_ge(S["x_dt_made"], c + 1)
                    pe.wait_ge(S["weighed_made"], 2 * (c + 1))
                    pe.wait_ge(S["y_off_made"], 2 * (c + 1))
                    for h in range(SSM_HEADS):
                        at = (h % HEADS_PER_GROUP) * HEAD_DIM
                        last = pe.matmul(ps_y[h // HEADS_PER_GROUP][:, at:at + HEAD_DIM], decay[:, h, :], x_dt[:, h, :],
                                         start=True, stop=True)
                    last.then_inc(S["diag_done"], 1)
                    if has(c - 1):
                        project(c - 1, 1, "attention")
                        project(c - 1, 1, "scan")
                    pe.wait_ge(S["y_scaled"], 2 * (c + 1))
                    pe.wait_ge(S["state_made"], c + 1)
                    for kk in range(KA):
                        last = pe.transpose(ps_turn[kk // 4][:, (kk % 4) * P:(kk % 4 + 1) * P],
                                            y_flat[:, kk * P:(kk + 1) * P], ident[:, :])
                    last.then_inc(S["y_turned"], 1)

                chunks(pe, body)
                for h in range(2):
                    project(CHUNKS - 1, h, "attention")
                    project(CHUNKS - 1, h, "scan")


def hybrid_layer_kernel(nc, x, norm_pre_w, w_in, conv_w, conv_b, dt_bias, a_log, d_skip, ssm_norm_w, w_out,
                        norm_post_w, out):
    def scratch(name, shape):
        return nc.dram_tensor(name, shape, F32, kind="Internal").ap()

    dram = {
        "feat": scratch("feat", (FT * P, SEQ)),
        "tok": scratch("tok", (SEQ, FT * P)),
        "dt": scratch("dt_scratch", (SSM_HEADS, SEQ)),
        "cum": scratch("cum_scratch", (SSM_HEADS, SEQ)),
        "attn": scratch("attn", (D_ATTN, SEQ)),
    }
    project(nc, dram, x[0], norm_pre_w, w_in[0], conv_w[0], conv_b)
    with nc.sbuf_tensor("cum_tok", [P, CHUNKS, SSM_HEADS], F32) as cum_tok, \
         nc.sbuf_tensor("dt_tok", [P, CHUNKS, SSM_HEADS], F32) as dt_tok:
        attend(nc, dram, dt_bias, a_log, cum_tok, dt_tok)
        scan_and_project(nc, dram, cum_tok, dt_tok, x[0], w_out[0], d_skip, ssm_norm_w, norm_post_w, out[0])


_INS = ["x", "norm_pre_w", "w_in", "conv_w", "conv_b", "dt_bias", "a_log", "d_skip", "ssm_norm_w", "w_out",
        "norm_post_w"]


def kernel(**inputs):
    import numpy as _np
    import concourse.bacc as _bacc
    from concourse import mybir as _mybir
    from concourse.bass_utils import run_bass_kernel_spmd as _run

    nc = _bacc.Bacc("TRN2", target_bir_lowering=False, num_devices=1)
    arrays, args = {}, []
    for name in _INS:
        a = _np.ascontiguousarray(inputs[name])
        arrays[f"in_{name}_dram"] = a
        args.append(nc.dram_tensor(f"in_{name}_dram", a.shape, _mybir.dt.from_np(a.dtype), kind="ExternalInput").ap())
    args.append(nc.dram_tensor("out_dram", (1, SEQ, D_MODEL), F32, kind="ExternalOutput").ap())
    hybrid_layer_kernel(nc, *args)
    r = _run(nc, [arrays], core_ids=[0])
    return r.results[0]["out_dram"]
```
